# Optimizing a Trainium2 kernel written in Bass

```python
import math
import jax, jax.numpy as jnp
from jax import lax
import numpy as np

D_MODEL = 1024
BATCH = 1
SEQ = 512
DEPTH = 2

N_EVEN = (DEPTH + 1) // 2
N_ODD = DEPTH // 2

S5_WIDTH = D_MODEL // 2
S5_GROUP = 16
S5_GROUPS = S5_WIDTH // S5_GROUP
S5_STATE = 64
S5_DT_MIN = 1e-3
S5_DT_MAX = 1e-1
CONV_WIDTH = D_MODEL // 2
CONV_K = 31
MIX_IN = S5_WIDTH + 2 * CONV_WIDTH
MIX_WIDTH = S5_WIDTH + CONV_WIDTH

HEAD_DIM = 64
N_Q_HEADS = D_MODEL // HEAD_DIM
N_KV_HEADS = 2
Q_PER_KV = N_Q_HEADS // N_KV_HEADS
QKV_WIDTH = (N_Q_HEADS + 2 * N_KV_HEADS) * HEAD_DIM
WINDOW = 128
ROPE_THETA = 500000.0
ROPE_DIM = HEAD_DIM // 4

PEER_HEADS = 8
PEER_N_KEYS = 128
PEER_N_EXPERTS = PEER_N_KEYS * PEER_N_KEYS
PEER_QUERY_DIM = 256
PEER_HALF = PEER_QUERY_DIM // 2
PEER_TOPK = 16
PEER_TOKEN_BLOCK = 128

NORM_EPS = 1e-6

kernel_name = "hybrid_s5_conv_swa_peer"

def rmsnorm(x, g):
    xf = x.astype(jnp.float32)
    y = xf * lax.rsqrt(jnp.mean(xf * xf, axis=-1, keepdims=True) + NORM_EPS) * g.astype(jnp.float32)
    return y.astype(x.dtype)

def s5_mixer(u, lam_re, lam_im, log_step, b_re, b_im, c_re, c_im, d, w_glu):
    bsz, seq, _ = u.shape
    uf = u.astype(jnp.float32).reshape(bsz, seq, S5_GROUPS, S5_GROUP)
    lam = lax.complex(lam_re.astype(jnp.float32), lam_im.astype(jnp.float32))
    dt = jnp.exp(log_step.astype(jnp.float32))[:, None]
    a_bar = jnp.exp(lam * dt)
    b = lax.complex(b_re.astype(jnp.float32), b_im.astype(jnp.float32))
    b_bar = ((a_bar - 1.0) / lam)[..., None] * b
    bu = lax.complex(jnp.einsum('blgh,gph->blgp', uf, jnp.real(b_bar)),
                     jnp.einsum('blgh,gph->blgp', uf, jnp.imag(b_bar)))
    a_seq = jnp.broadcast_to(a_bar, (1, seq) + a_bar.shape)

    def combine(left, right):
        a_l, b_l = left
        a_r, b_r = right
        return a_r * a_l, a_r * b_l + b_r

    _, h = lax.associative_scan(combine, (a_seq, bu), axis=1)
    y = (jnp.einsum('blgp,ghp->blgh', jnp.real(h), c_re.astype(jnp.float32))
         - jnp.einsum('blgp,ghp->blgh', jnp.imag(h), c_im.astype(jnp.float32))
         + d.astype(jnp.float32) * uf)
    y = jax.nn.gelu(y, approximate=False).reshape(bsz, seq, S5_WIDTH)
    out = y * jax.nn.sigmoid(y @ w_glu.astype(jnp.float32))
    return out.astype(u.dtype)

def conv_module(z, dw_w, dw_b, ln_g, ln_b):
    val, gate = jnp.split(z, 2, axis=-1)
    v = val * jax.nn.sigmoid(gate)
    y = lax.conv_general_dilated(v, dw_w[:, None, :], window_strides=(1,),
                                 padding=[(CONV_K - 1, 0)],
                                 dimension_numbers=('NWC', 'WIO', 'NWC'),
                                 feature_group_count=CONV_WIDTH) + dw_b
    yf = y.astype(jnp.float32)
    mu = jnp.mean(yf, axis=-1, keepdims=True)
    var = jnp.mean(jnp.square(yf - mu), axis=-1, keepdims=True)
    yn = (yf - mu) * lax.rsqrt(var + NORM_EPS) * ln_g.astype(jnp.float32) + ln_b.astype(jnp.float32)
    return jax.nn.silu(yn).astype(z.dtype)

def partial_rope(t, pos):
    inv = jnp.power(ROPE_THETA, -jnp.arange(0, ROPE_DIM, 2, dtype=jnp.float32) / ROPE_DIM)
    ang = pos[:, None] * inv[None, :]
    cos = jnp.cos(ang)[None, :, None, :]
    sin = jnp.sin(ang)[None, :, None, :]
    tr = t[..., :ROPE_DIM].astype(jnp.float32)
    x1, x2 = tr[..., :ROPE_DIM // 2], tr[..., ROPE_DIM // 2:]
    rot = jnp.concatenate([x1 * cos - x2 * sin, x2 * cos + x1 * sin], axis=-1).astype(t.dtype)
    return jnp.concatenate([rot, t[..., ROPE_DIM:]], axis=-1)

def sliding_window_attention(h, w_qkv, b_qkv, sinks, w_o):
    bsz, seq, _ = h.shape
    qkv = h @ w_qkv + b_qkv
    q, k, v = jnp.split(qkv, [N_Q_HEADS * HEAD_DIM, (N_Q_HEADS + N_KV_HEADS) * HEAD_DIM], axis=-1)
    pos = jnp.arange(seq, dtype=jnp.float32)
    q = partial_rope(q.reshape(bsz, seq, N_Q_HEADS, HEAD_DIM), pos)
    k = partial_rope(k.reshape(bsz, seq, N_KV_HEADS, HEAD_DIM), pos)
    v = v.reshape(bsz, seq, N_KV_HEADS, HEAD_DIM)
    nb = seq // WINDOW
    q = q.reshape(bsz, nb, WINDOW, N_KV_HEADS, Q_PER_KV, HEAD_DIM)
    k = k.reshape(bsz, nb, WINDOW, N_KV_HEADS, HEAD_DIM)
    v = v.reshape(bsz, nb, WINDOW, N_KV_HEADS, HEAD_DIM)

    def with_prev(t):
        prev = jnp.pad(t[:, :-1], ((0, 0), (1, 0), (0, 0), (0, 0), (0, 0)))
        return jnp.concatenate([prev, t], axis=2)

    kb, vb = with_prev(k), with_prev(v)
    s = jnp.einsum('bnqkgd,bnskd->bnkgqs', q, kb,
                   preferred_element_type=jnp.float32) * (HEAD_DIM ** -0.5)
    qi = jnp.arange(WINDOW)[:, None]
    si = jnp.arange(2 * WINDOW)[None, :]
    diff = WINDOW + qi - si
    band = (diff >= 0) & (diff < WINDOW)
    has_prev = (jnp.arange(nb)[:, None, None] > 0) | (si[None] >= WINDOW)
    valid = band[None] & has_prev
    s = jnp.where(valid[None, :, None, None], s, -jnp.inf)
    sink = sinks.astype(jnp.float32).reshape(N_KV_HEADS, Q_PER_KV)[None, None, :, :, None, None]
    m = jnp.maximum(jnp.max(s, axis=-1, keepdims=True), sink)
    p = jnp.exp(s - m)
    denom = jnp.sum(p, axis=-1, keepdims=True) + jnp.exp(sink - m)
    probs = (p / denom).astype(vb.dtype)
    o = jnp.einsum('bnkgqs,bnskd->bnqkgd', probs, vb)
    o = o.reshape(bsz, seq, N_Q_HEADS * HEAD_DIM).astype(h.dtype)
    return o @ w_o

def peer(h, w_q, sub_keys, u_tab, v_tab):
    bsz, seq, dm = h.shape
    t = bsz * seq
    hf = h.reshape(t, dm)
    q = (hf @ w_q).reshape(t, PEER_HEADS, 2, PEER_HALF)
    scores = jnp.einsum('thcd,hckd->thck', q, sub_keys,
                        preferred_element_type=jnp.float32)
    top_s, top_i = lax.top_k(scores, PEER_TOPK)
    cand_s = top_s[:, :, 0, :, None] + top_s[:, :, 1, None, :]
    cand_i = top_i[:, :, 0, :, None] * PEER_N_KEYS + top_i[:, :, 1, None, :]
    best_s, best_c = lax.top_k(cand_s.reshape(t, PEER_HEADS, PEER_TOPK * PEER_TOPK), PEER_TOPK)
    ids = jnp.take_along_axis(cand_i.reshape(t, PEER_HEADS, PEER_TOPK * PEER_TOPK), best_c, axis=-1)
    gates = jax.nn.softmax(best_s, axis=-1)
    n_exp = PEER_HEADS * PEER_TOPK
    nblk = t // PEER_TOKEN_BLOCK

    def token_block(args):
        xb, ib, gb = args
        u = jnp.take(u_tab, ib, axis=0)
        a = jnp.einsum('cd,ced->ce', xb, u, preferred_element_type=jnp.float32)
        w = (jax.nn.gelu(a, approximate=False) * gb).astype(v_tab.dtype)
        v = jnp.take(v_tab, ib, axis=0)
        return jnp.einsum('ce,ced->cd', w, v).astype(h.dtype)

    out = lax.map(token_block, (hf.reshape(nblk, PEER_TOKEN_BLOCK, dm),
                                ids.reshape(nblk, PEER_TOKEN_BLOCK, n_exp),
                                gates.reshape(nblk, PEER_TOKEN_BLOCK, n_exp)))
    return out.reshape(bsz, seq, dm)

def setup_inputs(seed: int = 0) -> dict:
    key = jax.random.key(seed)
    ks = iter(jax.random.split(key, 40))
    f32 = jnp.float32

    def nrm(shape, scale):
        return jax.random.normal(next(ks), shape, f32) * scale

    x = nrm((BATCH, SEQ, D_MODEL), 1.0)
    norm_mix = 1.0 + nrm((DEPTH, D_MODEL), 0.02)
    norm_ffn = 1.0 + nrm((DEPTH, D_MODEL), 0.02)
    norm_final = 1.0 + nrm((D_MODEL,), 0.02)
    mix_w_in = nrm((N_EVEN, D_MODEL, MIX_IN), D_MODEL ** -0.5)
    s5_lambda_re = -0.5 + nrm((N_EVEN, S5_GROUPS, S5_STATE), 0.01)
    s5_lambda_im = jnp.pi * jnp.arange(S5_STATE, dtype=f32) + nrm((N_EVEN, S5_GROUPS, S5_STATE), 0.01)
    s5_log_step = math.log(S5_DT_MIN) + jax.random.uniform(next(ks), (N_EVEN, S5_GROUPS), f32) * (
        math.log(S5_DT_MAX) - math.log(S5_DT_MIN))
    s5_b_re = nrm((N_EVEN, S5_GROUPS, S5_STATE, S5_GROUP), (2.0 * S5_GROUP) ** -0.5)
    s5_b_im = nrm((N_EVEN, S5_GROUPS, S5_STATE, S5_GROUP), (2.0 * S5_GROUP) ** -0.5)
    s5_c_re = nrm((N_EVEN, S5_GROUPS, S5_GROUP, S5_STATE), 0.5)
    s5_c_im = nrm((N_EVEN, S5_GROUPS, S5_GROUP, S5_STATE), 0.5)
    s5_d = nrm((N_EVEN, S5_GROUPS, S5_GROUP), 1.0)
    s5_w_glu = nrm((N_EVEN, S5_WIDTH, S5_WIDTH), S5_WIDTH ** -0.5)
    conv_dw_w = nrm((N_EVEN, CONV_K, CONV_WIDTH), CONV_K ** -0.5)
    conv_dw_b = nrm((N_EVEN, CONV_WIDTH), 0.01)
    conv_ln_g = 1.0 + nrm((N_EVEN, CONV_WIDTH), 0.02)
    conv_ln_b = nrm((N_EVEN, CONV_WIDTH), 0.01)
    mix_w_out = nrm((N_EVEN, MIX_WIDTH, D_MODEL), MIX_WIDTH ** -0.5)
    attn_w_qkv = nrm((N_ODD, D_MODEL, QKV_WIDTH), D_MODEL ** -0.5)
    attn_b_qkv = nrm((N_ODD, QKV_WIDTH), 0.01)
    attn_sinks = nrm((N_ODD, N_Q_HEADS), 0.5)
    attn_w_o = nrm((N_ODD, N_Q_HEADS * HEAD_DIM, D_MODEL), (N_Q_HEADS * HEAD_DIM) ** -0.5)
    peer_w_q = nrm((DEPTH, D_MODEL, PEER_HEADS * PEER_QUERY_DIM), D_MODEL ** -0.5)
    peer_sub_keys = nrm((DEPTH, PEER_HEADS, 2, PEER_N_KEYS, PEER_HALF), PEER_HALF ** -0.5)
    peer_u = nrm((DEPTH, PEER_N_EXPERTS, D_MODEL), D_MODEL ** -0.5)
    peer_v = nrm((DEPTH, PEER_N_EXPERTS, D_MODEL), 0.3)
    return {
        'x': x, 'norm_mix': norm_mix, 'norm_ffn': norm_ffn, 'norm_final': norm_final,
        'mix_w_in': mix_w_in, 's5_lambda_re': s5_lambda_re, 's5_lambda_im': s5_lambda_im,
        's5_log_step': s5_log_step, 's5_b_re': s5_b_re, 's5_b_im': s5_b_im,
        's5_c_re': s5_c_re, 's5_c_im': s5_c_im, 's5_d': s5_d, 's5_w_glu': s5_w_glu,
        'conv_dw_w': conv_dw_w, 'conv_dw_b': conv_dw_b, 'conv_ln_g': conv_ln_g, 'conv_ln_b': conv_ln_b,
        'mix_w_out': mix_w_out, 'attn_w_qkv': attn_w_qkv, 'attn_b_qkv': attn_b_qkv,
        'attn_sinks': attn_sinks, 'attn_w_o': attn_w_o, 'peer_w_q': peer_w_q,
        'peer_sub_keys': peer_sub_keys, 'peer_u': peer_u, 'peer_v': peer_v,
    }

def reference(x, norm_mix, norm_ffn, norm_final, mix_w_in, s5_lambda_re, s5_lambda_im,
              s5_log_step, s5_b_re, s5_b_im, s5_c_re, s5_c_im, s5_d, s5_w_glu,
              conv_dw_w, conv_dw_b, conv_ln_g, conv_ln_b, mix_w_out, attn_w_qkv, attn_b_qkv,
              attn_sinks, attn_w_o, peer_w_q, peer_sub_keys, peer_u, peer_v):
    for layer in range(DEPTH):
        i = layer // 2
        h = rmsnorm(x, norm_mix[layer])
        if layer % 2 == 0:
            z = h @ mix_w_in[i]
            y_ssm = s5_mixer(z[..., :S5_WIDTH], s5_lambda_re[i], s5_lambda_im[i], s5_log_step[i],
                             s5_b_re[i], s5_b_im[i], s5_c_re[i], s5_c_im[i], s5_d[i], s5_w_glu[i])
            y_conv = conv_module(z[..., S5_WIDTH:], conv_dw_w[i], conv_dw_b[i], conv_ln_g[i], conv_ln_b[i])
            x = x + jnp.concatenate([y_ssm, y_conv], axis=-1) @ mix_w_out[i]
        else:
            x = x + sliding_window_attention(h, attn_w_qkv[i], attn_b_qkv[i], attn_sinks[i], attn_w_o[i])
        x = x + peer(rmsnorm(x, norm_ffn[layer]), peer_w_q[layer], peer_sub_keys[layer],
                     peer_u[layer], peer_v[layer])
    return rmsnorm(x, norm_final)


_drawn_inputs = setup_inputs


def setup_inputs(seed=0):
    import zlib

    import numpy as np

    out = dict(_drawn_inputs(seed))
    spreads = {}
    factors = {'norm_final': 3.007,
     's5_lambda_re': 6.11,
     'conv_ln_b': 3.48,
     'attn_b_qkv': 3.421,
     'attn_sinks': 8.0}
    for name, (base, spread) in spreads.items():
        noise = np.random.default_rng([zlib.crc32(name.encode()), seed]).standard_normal(out[name].shape)
        drawn = base * np.exp(spread * noise) if base else spread * noise
        out[name] = __import__('jax').numpy.asarray(drawn.astype(out[name].dtype))
    for name, factor in factors.items():
        out[name] = (out[name] * factor).astype(out[name].dtype)
    return out
```

```python
import concourse.bass as bass
from concourse import mybir
from concourse.alu_op_type import AluOpType
from contextlib import ExitStack
import math
import numpy as np

P = 128
F32 = mybir.dt.float32
I32 = mybir.dt.int32
U32 = mybir.dt.uint32
ALU = AluOpType
ACT = mybir.ActivationFunctionType
AX_X = mybir.AxisListType.X

SEQ, DM = 512, 1024
NB = SEQ // P
KD = DM // P
EPS = 1e-6
S5_W, S5_G, S5_H, S5_P = 512, 32, 16, 64
NST = S5_G * S5_P // P
UT = S5_W // P
CONV_K = 31
NH, NKV, HD, ROT = 16, 2, 64, 8
QKV = (NH + 2 * NKV) * HD
NEG = -1.0e30
PH, PK, TOPK = 8, 128, 16
NEXP = PK * PK
NQT = 2 * PH


class Chain:

    def __init__(self, eng, sem):
        self.eng, self.sem, self.n = eng, sem, 0

    def link(self, ins):
        self.n += 1
        ins.then_inc(self.sem, 1)
        self.eng.wait_ge(self.sem, self.n)


class Sems:

    def __init__(self, nc, ctx, tag):
        self.nc, self.ctx, self.tag, self.made = nc, ctx, tag, []

    def __call__(self, name):
        s = self.nc.alloc_semaphore(self.tag + name)
        self.made.append(s)
        return s

    def block(self):
        self.ctx.callback(self.clear)
        return self.ctx.enter_context(self.nc.Block())

    def clear(self):
        self.nc.clear_and_free_semaphores(self.made)
        self.nc.all_engine_barrier()


def bc(ap, shape):
    return ap.broadcast_to(shape)



def norm_act(act, N):
    act.wait_ge(N.x_loaded, N.x_loaded_at)
    for b in range(NB):
        act.activation(N.h[:, b, :], N.x[:, b, :], ACT.Square,
                       accum_out=N.stat[:, b:b + 1]).then_inc(N.squares, 1)
    act.wait_ge(N.mean_ready, 1)
    act.activation(N.stat[:, 8:8 + NB], N.stat[:, 4:4 + NB], ACT.Sqrt).then_inc(N.root, 1)
    for n in range(2 * NB if N.hT is not None else 0):
        b, half = n // 2, n % 2
        act.wait_ge(N.turned, n + 1)
        act.copy(N.hT[:, 4 * half:4 * half + 4, b * P:(b + 1) * P], N.tp[n % 2]).then_inc(N.hT_ready, 1)


def norm_dve(dve, N):
    dve.wait_ge(N.squares, NB)
    dve.tensor_scalar(N.stat[:, 4:4 + NB], N.stat[:, 0:NB], 1.0 / DM, EPS, ALU.mult, ALU.add)\
       .then_inc(N.mean_ready, 1)
    dve.wait_ge(N.root, 1)
    dve.reciprocal(N.stat[:, 12:12 + NB], N.stat[:, 8:8 + NB]).then_inc(N.rstd_ready, 1)
    dve.wait_ge(N.rstd_ready, 1)
    dve.wait_ge(N.g_loaded, 16)
    for b in range(NB):
        dve.scalar_tensor_tensor(N.h[:, b, :], N.x[:, b, :], N.stat[:, 12 + b:13 + b], N.g[:, :],
                                 ALU.mult, ALU.mult).then_inc(N.h_ready, 1)


def norm_pe(pe, N):
    pe.wait_ge(N.ident_loaded, N.ident_loaded_at)
    for n in range(2 * NB):
        b, half = n // 2, n % 2
        if half == 0:
            pe.wait_ge(N.h_ready, b + 1)
        if n >= 2:
            pe.wait_ge(N.hT_ready, n - 1)
        for q in range(4):
            k = 4 * half + q
            mm = pe.transpose(N.tp[n % 2][:, q, :], N.h[:, b, k * P:(k + 1) * P], N.ident)
        mm.then_inc(N.turned, 1)


class Norm:

    def __init__(self, sem, tag, x, h, hT, stat, g, tp, ident):
        self.x, self.h, self.hT, self.stat, self.g, self.tp, self.ident = x, h, hT, stat, g, tp, ident
        self.squares, self.mean_ready = sem(tag + "_squares"), sem(tag + "_mean_ready")
        self.root, self.rstd_ready = sem(tag + "_root"), sem(tag + "_rstd_ready")
        self.g_loaded, self.h_ready = sem(tag + "_g_loaded"), sem(tag + "_h_ready")
        self.turned, self.hT_ready = sem(tag + "_turned"), sem(tag + "_hT_ready")
        self.x_loaded_at = 0
        self.ident_loaded_at = 0



def hybrid_mixer(nc, D, x, ident, loaded, iota):
    with ExitStack() as ctx:
        def sb(name, shape, dt=F32):
            return ctx.enter_context(nc.sbuf_tensor(name, shape, dt))

        sem = Sems(nc, ctx, "m0_")

        late = sb("m0_late", [P, 8, SEQ])
        h = late[:, :, :].rearrange("p (b two) t -> p b (two t)", two=2)
        yg, cv = late[:, 0:4, :], late[:, 4:8, :]
        hT = sb("m0_hT", [P, KD, SEQ])
        wring = sb("m0_wring", [P, 4, 1024])
        uT = sb("m0_uT", [P, UT, SEQ])
        PAD = CONV_K - 1
        vpad = sb("m0_vpad", [P, UT, PAD + SEQ])
        gsg = sb("m0_gsg", [P, 2, SEQ])
        g = gsg[:, :, :].rearrange("p a t -> p (a t)")
        ec = sb("m0_ec", [P, NST, SEQ])
        es = sb("m0_es", [P, NST, SEQ])
        work = sb("m0_work", [P, 16, SEQ])
        tmp_c = work[:, 0:4, :].rearrange("p a t -> p (a t)")
        tmp_s = work[:, 4:8, :].rearrange("p a t -> p (a t)")
        rot = work[:, 0:4, :]
        st = work[:, 4:8, :].rearrange("p (b r) t -> p b r t", b=2)
        pr = work[:, 8:16, :].rearrange("p (b r) t -> p b r t", b=2)
        diag = sb("m0_diag", [P, 8, P])
        bT = sb("m0_bT", [P, 2, UT, P])
        cT = sb("m0_cT", [P, 2, NST, 32])
        cc = sb("m0_cc", [P, 4, NST, 32])
        sp = sb("m0_sp", [P, 3, NST])
        pv = sb("m0_pv", [P, 40, NST])
        pw = sb("m0_pw", [P, 2, 9, NST])
        dcol = sb("m0_dcol", [P, 4, UT])
        cw = sb("m0_cw", [P, UT, CONV_K])
        ones = sb("m0_ones", [P, P])
        stat = sb("m0_stat", [P, 16])

        bank = [ctx.enter_context(nc.psum_tensor(f"m0_ps{i}", [P, SEQ], F32)) for i in range(8)]
        tp = [bank[6][:, :].rearrange("p (a b) -> p a b", a=4), bank[7][:, :].rearrange("p (a b) -> p a b", a=4)]

        s_par = sem("params_loaded")
        s_win = [sem(f"weight_tile{i}_loaded") for i in range(4)]
        s_wuse = sem("weight_tiles_used")
        s_chain = sem("dve_chain")
        s_sin_in = sem("angle_reduced")
        s_sin = sem("sines_ready")
        s_pow = sem("powers_ready")
        s_first = sem("tables_started")
        s_ec, s_es = sem("cos_table_level"), sem("sin_table_level")
        s_poolc = sem("pool_chain")
        s_coef = sem("c_scaled")
        s_z = sem("z_tile_done")
        s_zact, s_zdve = sem("z_tile_taken_by_act"), sem("z_tile_taken_by_dve")
        s_sg, s_pad = sem("gate_sigmoid_ready"), sem("pad_zeroed")
        s_v = sem("input_products_ready")
        s_vused = sem("input_products_taken")
        s_state = sem("states_scanned")
        s_pd, s_pp = sem("products_by_dve"), sem("products_by_pool")
        s_cmm = sem("state_tile_projected")
        s_yd, s_yg = sem("y_with_skip_ready"), sem("y_gelu_ready")
        s_diag = sem("tap_diagonal_ready")
        s_tap = sem("tap_done")
        s_cv = sem("conv_tile_taken")
        s_ones = sem("ones_ready")
        s_mean, s_cen, s_sq = sem("mean_ready"), sem("centred_ready"), sem("centred_squared")
        s_var, s_vr, s_sd, s_rs, s_yn = sem("var_ready"), sem("var_eps_ready"), sem("std_ready"), sem("rstd_ready"), sem("ln_scaled")
        s_lnout = sem("conv_branch_ready")
        s_glu, s_gs, s_sout = sem("glu_done"), sem("glu_sigmoid_ready"), sem("s5_branch_ready")
        s_o, s_xr = sem("out_block_done"), sem("residual_added")
        s_iota = sem("iota_ready")
        N = Norm(sem, "n", x, h, hT, stat, g, tp, ident[:, :])
        N.x_loaded, N.x_loaded_at = loaded, 32
        N.ident_loaded, N.ident_loaded_at = loaded, 32

        NZ = 12
        zcol = [0, 1, 2, 3] + [c for i in range(UT) for c in (8 + i, 4 + i)]
        win = D["w_in"].rearrange("(k p) (n c) -> n p k c", p=P, c=P)
        wglu = D["w_glu"].rearrange("(k p) c -> p k c", p=P)
        wout = D["w_out"].rearrange("(k p) c -> k p c", p=P)

        block = sem.block()

        def skip(dve, c):
            dve.wait_ge(s_cmm, 4 * (c + 1))
            dve.scalar_tensor_tensor(yg[:, c, :], uT[:, c, :], dcol[:, 0, c:c + 1], bank[4 + c % 2][:, :],
                                     ALU.mult, ALU.add).then_inc(s_yd, 1)

        @block.sync
        def _(sp_):
            sp_.dma_start(x[:, :, :], D["x"].rearrange("(b p) d -> p b d", p=P)).then_inc(loaded, 16)
            sp_.dma_start(ident[:, :], D["ident"]).then_inc(loaded, 16)
            sp_.dma_start(g, D["g_mix"][0:1, :].to_broadcast([P, DM])).then_inc(N.g_loaded, 16)
            for dst, src in ((sp[:, :, :], D["s5_scal"]), (bT[:, :, :, :], D["s5_bT"]), (cT[:, :, :, :], D["s5_cT"]),
                             (dcol[:, :, :], D["chan_cols"]), (cw[:, :, :], D["conv_w"])):
                sp_.dma_start(dst, src).then_inc(s_par, 16)
            for n in range(NZ + 2 + KD):
                if n >= 4:
                    sp_.wait_ge(s_wuse, n - 3)
                slot = wring[:, n % 4, :]
                if n < NZ:
                    dst, src = slot.rearrange("p (k c) -> p k c", k=KD), win[zcol[n]]
                elif n < NZ + 2:
                    dst, src = slot.rearrange("p (k c) -> p k c", k=2), wglu[:, 2 * (n - NZ):2 * (n - NZ) + 2, :]
                else:
                    dst, src = slot, wout[n - NZ - 2]
                sp_.dma_start(dst, src).then_inc(s_win[n % 4], 16)

        @block.gpsimd
        def _(pool):
            pool.memset(ones[:, :], 1.0 / S5_W).then_inc(s_ones, 1)
            pool.iota(iota[:, :], pattern=[[1, TOPK]], base=0, channel_multiplier=0,
                      allow_small_or_imprecise_dtypes=True).then_inc(s_iota, 1)
            pool.wait_ge(s_iota, 1)
            pool.memset(vpad[:, :, 0:PAD], 0.0).then_inc(s_pad, 1)
            ch = Chain(pool, s_poolc)
            pool.wait_ge(s_pow, 1)
            pool.wait_ge(s_first, 2)
            for j in range(9):
                n = 1 << j
                for a, m in ([(0, n)] if n <= 128 else [(o, 128) for o in range(0, n, 128)]):
                    t = tmp_s[:, 0:NST * m].rearrange("p (k t) -> p k t", k=NST)
                    pc = bc(pw[:, 0, j, :].unsqueeze(2), [P, NST, m])
                    ps = bc(pw[:, 1, j, :].unsqueeze(2), [P, NST, m])
                    pool.wait_ge(s_ec, j)
                    pool.wait_ge(s_es, j)
                    pool.tensor_tensor(es[:, :, n + a:n + a + m], es[:, :, a:a + m], pc, ALU.mult).then_inc(s_poolc, 1)
                    pool.tensor_tensor(t, ec[:, :, a:a + m], ps, ALU.mult).then_inc(s_poolc, 1)
                    ch.n += 2
                    pool.wait_ge(s_poolc, ch.n)
                    ch.link(pool.tensor_tensor(es[:, :, n + a:n + a + m], es[:, :, n + a:n + a + m], t, ALU.add))
                pool.sem_inc(s_es, 1)
            done = 0
            def make_diag(upto):
                nonlocal done
                for q in range(done, upto):
                    if q >= 8:
                        pool.wait_ge(s_tap, q - 7)
                    pool.tensor_scalar(diag[:, q % 8, :], ident[:, :], cw[:, q // CONV_K, q % CONV_K:q % CONV_K + 1], 1.0,
                                       ALU.mult, ALU.mult).then_inc(s_diag, 1)
                done = upto
            pool.wait_ge(s_par, 80)
            for k in range(NST):
                make_diag(min(8 * (k + 1), UT * CONV_K))
                pool.wait_ge(s_state, 2 * (k + 1))
                if k >= 2:
                    pool.wait_ge(s_cmm, k - 1)
                pool.tensor_tensor(pr[:, k % 2, 1, :], st[:, k % 2, 0, :], es[:, k, :], ALU.mult).then_inc(s_pp, 1)
                pool.tensor_tensor(pr[:, k % 2, 3, :], st[:, k % 2, 1, :], es[:, k, :], ALU.mult).then_inc(s_pp, 1)

        @block.scalar
        def _(act):
            norm_act(act, N)
            act.wait_ge(s_sin_in, 1)
            act.activation(pv[:, 20, :], pv[:, 15, :], ACT.Sin).then_inc(s_sin, 1)
            act.activation(pv[:, 21, :], pv[:, 15, :], ACT.Sin, scale=0.5).then_inc(s_sin, 1)
            for n in range(UT):
                act.wait_ge(s_z, n + 1)
                act.copy(uT[:, n, :], bank[n % 4][:, :]).then_inc(s_zact, 1)
            for i in range(UT):
                act.wait_ge(s_z, 4 + 2 * i + 1)
                if i >= 2:
                    act.wait_ge(s_zdve, i - 1)
                act.activation(gsg[:, i % 2, :], bank[(4 + 2 * i) % 4][:, :], ACT.Sigmoid).then_inc(s_zact, 1)
            for i in range(UT):
                act.wait_ge(s_tap, CONV_K * (i + 1))
                act.activation(cv[:, i, :], bank[6][:, :], ACT.Identity, bias=dcol[:, 1, i:i + 1]).then_inc(s_cv, 1)
                act.wait_ge(s_yd, i + 1)
                act.activation(yg[:, i, :], yg[:, i, :], ACT.Gelu).then_inc(s_yg, 1)
            for i in range(UT):
                act.wait_ge(s_cen, i + 1)
                act.activation(rot[:, i, :], cv[:, i, :], ACT.Square).then_inc(s_sq, 1)
            for i in range(UT):
                act.wait_ge(s_glu, i + 1)
                if i >= 2:
                    act.wait_ge(s_sout, i - 1)
                act.activation(gsg[:, i % 2, :], bank[i % 4][:, :], ACT.Sigmoid).then_inc(s_gs, 1)
            act.wait_ge(s_vr, 1)
            act.activation(st[:, 0, 0, :], st[:, 0, 1, :], ACT.Sqrt).then_inc(s_sd, 1)
            for i in range(UT):
                act.wait_ge(s_yn, i + 1)
                act.activation(hT[:, 4 + i, :], cv[:, i, :], ACT.Silu, bias=dcol[:, 3, i:i + 1],
                               scale=dcol[:, 2, i:i + 1]).then_inc(s_lnout, 1)

        @block.vector
        def _(dve):
            ch = Chain(dve, s_chain)

            def V(i):
                return pv[:, i, :]

            def ts(o, a, s1, s2, op0, op1=ALU.bypass):
                ch.link(dve.tensor_scalar(o, a, s1, s2, op0, op1))

            def tt(o, a, b, op):
                ch.link(dve.tensor_tensor(o, a, b, op))

            def stt(o, a, s, b, op0, op1):
                ch.link(dve.scalar_tensor_tensor(o, a, s, b, op0, op1))

            MAGIC = 12582912.0

            def exp_small(o, a, n, r, t):
                ts(t, a, -87.0, 88.0, ALU.max, ALU.min)
                ts(n, t, 1.0 / math.log(2.0), MAGIC, ALU.mult, ALU.add)
                ts(n, n, MAGIC, None, ALU.subtract)
                stt(r, n, -0.693359375, t, ALU.mult, ALU.add)
                stt(r, n, 2.12194440e-4, r, ALU.mult, ALU.add)
                ts(t, r, 1.0 / math.factorial(8), None, ALU.mult)
                for q in range(7, 0, -1):
                    stt(t, t, 1.0 / math.factorial(q), r, ALU.add, ALU.mult)
                ts(t, t, 1.0, None, ALU.add)
                ts(n.bitcast(I32), n, 127.0, 8388608.0, ALU.add, ALU.mult)
                tt(o, t, n, ALU.mult)

            dve.wait_ge(s_par, 80)
            lre, lim = sp[:, 0, :], sp[:, 1, :]
            exp_small(V(0), sp[:, 2, :], V(1), V(2), V(3))
            tt(V(4), lre, V(0), ALU.mult)
            exp_small(V(5), V(4), V(6), V(7), V(8))
            tt(V(9), lim, V(0), ALU.mult)
            ts(V(10), V(9), 1.0 / (2 * math.pi), MAGIC, ALU.mult, ALU.add)
            ts(V(11), V(10), MAGIC, None, ALU.subtract)
            c1 = 6.28125
            c2 = float(np.float32(2 * math.pi - c1))
            c3 = 2 * math.pi - c1 - c2
            stt(V(12), V(11), -c1, V(9), ALU.mult, ALU.add)
            stt(V(13), V(11), -c2, V(12), ALU.mult, ALU.add)
            stt(V(14), V(11), -c3, V(13), ALU.mult, ALU.add)
            dve.tensor_scalar(V(15), V(14), 3.1415925, -3.1415925, ALU.min, ALU.max).then_inc(s_sin_in, 1)

            norm_dve(dve, N)

            dve.wait_ge(s_sin, 2)
            stt(V(22), V(21), -2.0, V(21), ALU.mult, ALU.mult)
            ts(pw[:, 0, 0, :], V(22), 1.0, None, ALU.add)
            ts(pw[:, 1, 0, :], V(20), 1.0, None, ALU.mult)
            for j in range(8):
                tt(V(23), pw[:, 0, j, :], pw[:, 0, j, :], ALU.mult)
                tt(V(24), pw[:, 1, j, :], pw[:, 1, j, :], ALU.mult)
                tt(pw[:, 0, j + 1, :], V(23), V(24), ALU.subtract)
                stt(pw[:, 1, j + 1, :], pw[:, 0, j, :], 2.0, pw[:, 1, j, :], ALU.mult, ALU.mult)
            dve.memset(ec[:, :, 0:1], 1.0).then_inc(s_first, 1)
            dve.memset(es[:, :, 0:1], 0.0).then_inc(s_first, 1)
            dve.sem_inc(s_pow, 1)
            dve.wait_ge(s_first, 2)
            for j in range(9):
                n = 1 << j
                for a, m in ([(0, n)] if n <= 128 else [(o, 128) for o in range(0, n, 128)]):
                    t = tmp_c[:, 0:NST * m].rearrange("p (k t) -> p k t", k=NST)
                    pc = bc(pw[:, 0, j, :].unsqueeze(2), [P, NST, m])
                    ps = bc(pw[:, 1, j, :].unsqueeze(2), [P, NST, m])
                    dve.wait_ge(s_es, j)
                    dve.tensor_tensor(ec[:, :, n + a:n + a + m], ec[:, :, a:a + m], pc, ALU.mult).then_inc(s_chain, 1)
                    dve.tensor_tensor(t, es[:, :, a:a + m], ps, ALU.mult).then_inc(s_chain, 1)
                    ch.n += 2
                    dve.wait_ge(s_chain, ch.n)
                    tt(ec[:, :, n + a:n + a + m], ec[:, :, n + a:n + a + m], t, ALU.subtract)
                dve.sem_inc(s_ec, 1)

            ts(V(25), V(5), -1.0, None, ALU.add)
            tt(V(26), V(5), V(22), ALU.mult)
            tt(V(27), V(25), V(26), ALU.add)
            tt(V(28), V(5), V(20), ALU.mult)
            tt(V(29), lre, lre, ALU.mult)
            tt(V(30), lim, lim, ALU.mult)
            tt(V(31), V(29), V(30), ALU.add)
            ch.link(dve.reciprocal(V(32), V(31)))
            tt(V(33), V(27), lre, ALU.mult)
            tt(V(34), V(28), lim, ALU.mult)
            tt(V(35), V(33), V(34), ALU.add)
            tt(V(36), V(35), V(32), ALU.mult)
            tt(V(33), V(28), lre, ALU.mult)
            tt(V(34), V(27), lim, ALU.mult)
            tt(V(35), V(33), V(34), ALU.subtract)
            tt(V(37), V(35), V(32), ALU.mult)
            kr = bc(V(36).unsqueeze(2), [P, NST, 32])
            ki = bc(V(37).unsqueeze(2), [P, NST, 32])
            tt(cc[:, 3, :, :], cT[:, 1, :, :], ki, ALU.mult)
            tt(cc[:, 2, :, :], cT[:, 0, :, :], kr, ALU.mult)
            tt(cc[:, 0, :, :], cc[:, 2, :, :], cc[:, 3, :, :], ALU.subtract)
            tt(cc[:, 3, :, :], cT[:, 0, :, :], ki, ALU.mult)
            tt(cc[:, 2, :, :], cT[:, 1, :, :], kr, ALU.mult)
            stt(cc[:, 2, :, :], cc[:, 2, :, :], -1.0, cc[:, 3, :, :], ALU.mult, ALU.subtract)
            ts(cc[:, 1, :, :], cc[:, 0, :, :], -1.0, None, ALU.mult)
            dve.sem_inc(s_coef, 1)

            dve.wait_ge(s_pad, 1)
            for i in range(UT):
                dve.wait_ge(s_zact, UT + i + 1)
                dve.wait_ge(s_z, 4 + 2 * i + 2)
                dve.tensor_tensor(vpad[:, i, PAD:], bank[(5 + 2 * i) % 4][:, :], gsg[:, i % 2, :], ALU.mult)\
                   .then_inc(s_zdve, 1)

            dve.wait_ge(s_es, 9)
            for k in range(NST):
                mag = bc(pv[:, 5, k:k + 1], [P, SEQ])
                vre, vim = bank[2 * (k % 2)], bank[2 * (k % 2) + 1]
                dve.wait_ge(s_v, k + 1)
                dve.tensor_tensor(rot[:, 0, :], vre[:, :], ec[:, k, :], ALU.mult).then_inc(s_chain, 1)
                dve.tensor_tensor(rot[:, 1, :], vim[:, :], es[:, k, :], ALU.mult).then_inc(s_chain, 1)
                dve.tensor_tensor(rot[:, 2, :], vim[:, :], ec[:, k, :], ALU.mult).then_inc(s_chain, 1)
                dve.tensor_tensor(rot[:, 3, :], vre[:, :], es[:, k, :], ALU.mult).then_inc(s_chain, 1)
                dve.wait_ge(s_chain, ch.n + 2)
                dve.tensor_tensor(rot[:, 0, :], rot[:, 0, :], rot[:, 1, :], ALU.add).then_inc(s_chain, 1)
                dve.wait_ge(s_chain, ch.n + 4)
                dve.tensor_tensor(rot[:, 2, :], rot[:, 2, :], rot[:, 3, :], ALU.subtract).then_inc(s_chain, 1)
                dve.sem_inc(s_vused, 1)
                dve.wait_ge(s_chain, ch.n + 5)
                if k >= 2:
                    dve.wait_ge(s_pp, 2 * (k - 1))
                dve.tensor_tensor_scan(st[:, k % 2, 0, :], mag, rot[:, 0, :], 0.0, ALU.mult, ALU.add).then_inc(s_state, 1)
                dve.wait_ge(s_chain, ch.n + 6)
                dve.tensor_tensor_scan(st[:, k % 2, 1, :], mag, rot[:, 2, :], 0.0, ALU.mult, ALU.add).then_inc(s_state, 1)
                ch.n += 6
                if k >= 2:
                    dve.wait_ge(s_cmm, k - 1)
                dve.wait_ge(s_state, 2 * k + 1)
                dve.tensor_tensor(pr[:, k % 2, 0, :], st[:, k % 2, 0, :], ec[:, k, :], ALU.mult).then_inc(s_pd, 1)
                dve.wait_ge(s_state, 2 * k + 2)
                dve.tensor_tensor(pr[:, k % 2, 2, :], st[:, k % 2, 1, :], ec[:, k, :], ALU.mult).then_inc(s_pd, 1)
                if k % 4 == 0 and k:
                    skip(dve, k // 4 - 1)
            skip(dve, UT - 1)

            dve.wait_ge(s_mean, 1)
            for i in range(UT):
                dve.tensor_tensor(cv[:, i, :], cv[:, i, :], bank[6][:, :], ALU.subtract).then_inc(s_cen, 1)
            for i in range(UT):
                dve.wait_ge(s_gs, i + 1)
                dve.tensor_tensor(hT[:, i, :], yg[:, i, :], gsg[:, i % 2, :], ALU.mult).then_inc(s_sout, 1)
            dve.wait_ge(s_var, 1)
            dve.tensor_scalar(st[:, 0, 1, :], bank[7][:, :], EPS, None, ALU.add).then_inc(s_vr, 1)
            dve.wait_ge(s_sd, 1)
            dve.reciprocal(st[:, 1, 0, :], st[:, 0, 0, :]).then_inc(s_rs, 1)
            dve.wait_ge(s_rs, 1)
            for i in range(UT):
                dve.tensor_tensor(cv[:, i, :], cv[:, i, :], st[:, 1, 0, :], ALU.mult).then_inc(s_yn, 1)
            for n in range(2 * NB):
                dve.wait_ge(s_o, n + 1)
                b, half = n // 2, n % 2
                xs = x[:, b, half * 512:(half + 1) * 512]
                dve.tensor_tensor(xs, xs, bank[n][:, :], ALU.add).then_inc(s_xr, 1)
            dve.wait_ge(s_xr, 2 * NB)

        @block.tensor
        def _(pe):
            norm_pe(pe, N)
            pe.wait_ge(N.hT_ready, 2 * NB)
            for n in range(NZ):
                pe.wait_ge(s_win[n % 4], 16 * (n // 4 + 1))
                if n >= 4:
                    m = n - 4
                    if m < 4:
                        pe.wait_ge(s_zact, m + 1)
                    elif m % 2 == 0:
                        pe.wait_ge(s_zact, 4 + (m - 4) // 2 + 1)
                    else:
                        pe.wait_ge(s_zdve, (m - 5) // 2 + 1)
                w = wring[:, n % 4, :].rearrange("p (k c) -> p k c", k=KD)
                for k in range(KD):
                    mm = pe.matmul(bank[n % 4][:, :], w[:, k, :], hT[:, k, :], start=(k == 0), stop=(k == KD - 1))
                mm.then_inc(s_z, 1)
                pe.wait_ge(s_z, n + 1)
                pe.sem_inc(s_wuse, 1)

            def inputs(k):
                if k == 0:
                    pe.wait_ge(s_zact, 2 * UT)
                    pe.wait_ge(s_zdve, UT)
                if k >= 2:
                    pe.wait_ge(s_vused, k - 1)
                c, r = k // 4, 32 * (k % 4)
                for part in range(2):
                    mm = pe.matmul(bank[2 * (k % 2) + part][:, :], bT[r:r + 32, part, c, :], uT[r:r + 32, c, :],
                                   start=True, stop=True, tile_position=(r, 0))
                mm.then_inc(s_v, 1)

            pe.wait_ge(s_par, 80)
            inputs(0)
            taps = 0
            for k in range(NST):
                if k + 1 < NST:
                    inputs(k + 1)
                while taps < min(8 * (k + 1), UT * CONV_K):
                    i, j = taps // CONV_K, taps % CONV_K
                    if j == 0 and i:
                        pe.wait_ge(s_cv, i)
                    pe.wait_ge(s_diag, taps + 1)
                    pe.matmul(bank[6][:, :], diag[:, taps % 8, :], vpad[:, i, j:j + SEQ], start=(j == 0),
                              stop=(j == CONV_K - 1)).then_inc(s_tap, 1)
                    taps += 1
                c, r = k // 4, 32 * (k % 4)
                if k == 0:
                    pe.wait_ge(s_coef, 1)
                if k % 4 == 0 and c >= 2:
                    pe.wait_ge(s_yd, c - 1)
                pe.wait_ge(s_pd, 2 * (k + 1))
                pe.wait_ge(s_pp, 2 * (k + 1))
                for q, w in enumerate((0, 2, 2, 1)):
                    mm = pe.matmul(bank[4 + c % 2][r:r + 32, :], cc[:, w, k, :], pr[:, k % 2, q, :],
                                   start=(q == 0), stop=(q == 3), tile_position=(0, r))
                mm.then_inc(s_cmm, 1)

            pe.wait_ge(s_ones, 1)
            pe.wait_ge(s_cv, UT)
            for i in range(UT):
                mm = pe.matmul(bank[6][:, :], ones[:, :], cv[:, i, :], start=(i == 0), stop=(i == UT - 1))
            mm.then_inc(s_mean, 1)
            pe.wait_ge(s_yg, UT)
            for q in range(2):
                pe.wait_ge(s_win[(NZ + q) % 4], 16 * ((NZ + q) // 4 + 1))
            for i in range(UT):
                for k in range(UT):
                    w = wring[:, (NZ + k // 2) % 4, :].rearrange("p (k c) -> p k c", k=2)[:, k % 2, i * P:(i + 1) * P]
                    mm = pe.matmul(bank[i][:, :], w, yg[:, k, :], start=(k == 0), stop=(k == UT - 1))
                mm.then_inc(s_glu, 1)
            for i in range(UT):
                pe.wait_ge(s_sq, i + 1)
                mm = pe.matmul(bank[7][:, :], ones[:, :], rot[:, i, :], start=(i == 0), stop=(i == UT - 1))
            mm.then_inc(s_var, 1)
            pe.wait_ge(s_glu, UT)
            pe.sem_inc(s_wuse, 2)
            pe.wait_ge(s_sout, UT)
            pe.wait_ge(s_yn, UT)
            pe.wait_ge(s_lnout, UT)
            for k in range(KD):
                n = NZ + 2 + k
                pe.wait_ge(s_win[n % 4], 16 * (n // 4 + 1))
                for o in range(2 * NB):
                    b, half = o // 2, o % 2
                    mm = pe.matmul(bank[o][:, :], hT[:, k, b * P:(b + 1) * P],
                                   wring[:, n % 4, half * 512:(half + 1) * 512], start=(k == 0), stop=(k == KD - 1))
                    if k == KD - 1:
                        mm.then_inc(s_o, 1)
                if k < KD - 1:
                    mm.then_inc(s_wuse, 1)



def peer(nc, D, layer, x, ident, loaded, iota):
    tag = f"p{layer}_"
    R = 8
    with ExitStack() as ctx:
        def sb(name, shape, dt=F32):
            return ctx.enter_context(nc.sbuf_tensor(tag + name, shape, dt))

        def two(name, shape, dt=F32):
            return [sb(f"{name}{p}", shape, dt) for p in range(2)]

        sem = Sems(nc, ctx, tag)
        h = sb("h", [P, NB, DM])
        hT = sb("hT", [P, KD, SEQ])
        g = sb("g", [P, DM])
        stat = sb("stat", [P, 16])
        wq, keys = two("wq", [P, KD, P]), two("keys", [P, PK])
        qT = two("qT", [P, SEQ])
        S = sb("S", [P, NB, 2, PK])
        urow, vrow = sb("urow", [P, R, DM]), sb("vrow", [P, R, DM])
        diag = two("diag", [P, TOPK, P])
        sc2 = sb("sc2", [P, 2, PK])
        tops, topi = sb("tops", [P, 2, TOPK]), sb("topi", [P, 2, TOPK], U32)
        topf = sb("topf", [P, 2, TOPK])
        cand, cand2 = sb("cand", [P, TOPK, TOPK]), sb("cand2", [P, TOPK, TOPK])
        best, bestc = two("best", [P, TOPK]), sb("bestc", [P, TOPK], U32)
        ab, abf = sb("ab", [P, 2, TOPK], U32), sb("abf", [P, 2, TOPK])
        hit = sb("hit", [P, 2, TOPK, TOPK])
        sel, flat = sb("sel", [P, 2, TOPK]), sb("flat", [P, TOPK])
        idu, idv = two("idu", [P, TOPK], I32), two("idv", [P, TOPK], I32)
        negm, esum, e = two("negm", [P, 1]), two("esum", [P, 1]), two("e", [P, TOPK])
        a, ga, w, rs = two("a", [P, TOPK]), two("ga", [P, TOPK]), two("w", [P, TOPK]), two("rs", [P, 1])
        bankA = ctx.enter_context(nc.psum_tensor(tag + "psA", [P, SEQ], F32))
        bankB = ctx.enter_context(nc.psum_tensor(tag + "psB", [P, SEQ], F32))
        hp = ctx.enter_context(nc.psum_tensor(tag + "hp", [P, DM], F32))
        acc = [ctx.enter_context(nc.psum_tensor(f"{tag}acc{p}", [P, DM], F32)) for p in range(2)]
        tp = [bankA[:, :].rearrange("p (a b) -> p a b", a=4), bankB[:, :].rearrange("p (a b) -> p a b", a=4)]

        s_wqfree = sem("wq_buffers_used")
        s_wq = [sem(f"wq{c}_loaded") for c in range(2)]
        s_keys = [sem(f"keys{c}_loaded") for c in range(2)]
        s_q, s_qT = sem("query_tile_done"), sem("query_tile_taken")
        s_sd, s_S = sem("score_tile_done"), sem("score_tile_taken")
        s_ufree, s_vfree = sem("u_slots_free"), sem("v_slots_free")
        s_ug = [sem(f"u_rows{i}_landed") for i in range(R)]
        s_vg = [sem(f"v_rows{i}_landed") for i in range(R)]
        s_h = sem("h_staged")
        s_idu, s_idv = sem("u_indices_ready"), sem("v_indices_ready")
        s_best, s_exp = sem("best_scores_ready"), sem("exponents_ready")
        s_gelu, s_w = sem("gelu_ready"), sem("weights_ready")
        s_dgfree, s_dg = sem("diagonal_buffers_free"), sem("diagonals_ready")
        s_accfree, s_acc = sem("sum_buffers_free"), sem("sums_ready")
        s_chain = sem("dve_chain")
        s_tick = {n: sem(f"{n}_waits_passed") for n in ("pool", "dve", "act")}
        N = Norm(sem, "n", x, h, hT, stat, g, tp, ident[:, :])
        N.x_loaded, N.x_loaded_at = loaded, 32
        N.ident_loaded, N.ident_loaded_at = loaded, 32
        utab = D["peer_u"].rearrange("l e d -> (l e) d")
        vtab = D["peer_v"].rearrange("l e d -> (l e) d")
        wq_d = D["w_q"][layer].rearrange("n p c -> (n p) c")
        keys_d = D["keysT"][layer].rearrange("n p c -> (n p) c")

        def held(eng, name, s, value):
            eng.wait_ge(s, value)
            eng.sem_inc(s_tick[name], 1)

        block = sem.block()

        @block.sync
        def _(sp):
            def load(n, c, row):
                sp.dma_start(wq[c][:, :, :].rearrange("p k c -> p (k c)"), wq_d[row, :]).then_inc(s_wq[c], 16)
                sp.dma_start(keys[c][:, :], keys_d[row, :]).then_inc(s_keys[c], 16)

            sp.dma_start(g[:, :], D["g_ffn"][layer:layer + 1, :].to_broadcast([P, DM])).then_inc(N.g_loaded, 16)
            for c in range(2):
                load(c, c, slice(c * P, (c + 1) * P))
            with sp.Fori(0, PH - 1) as hd:
                for c in range(2):
                    sp.wait_ge(s_wqfree, 2 * hd + c + 1)
                    load(None, c, bass.ds((2 * hd + 2 + c) * P, P))

        @block.gpsimd
        def _(pool):
            def rows(p, k, slots, free, landed, ids, table, value):
                held(pool, "pool", free, value)
                pool.indirect_dma_start(slots[:, k % R, :], None, table,
                                        bass.IndirectOffsetOnAxis(ap=ids[p][:, k:k + 1], axis=0))\
                    .then_inc(landed[k % R], 16)

            def step(v, b, more):
                p = b % 2
                if more:
                    held(pool, "pool", s_idu, v + 2)
                held(pool, "pool", s_idv, v + 1)
                for k in range(TOPK):
                    if more:
                        rows(1 - p, k, urow, s_ufree, s_ug, idu, utab, 16 * v + 16 + k + 1)
                    rows(p, k, vrow, s_vfree, s_vg, idv, vtab, 16 * v + k + 1)

            pool.wait_ge(s_idu, 1)
            for k in range(TOPK):
                rows(0, k, urow, s_ufree, s_ug, idu, utab, k + 1)
            with pool.Fori(0, PH - 1) as hd:
                for b in range(NB):
                    step(4 * hd + b, b, True)
            for b in range(NB):
                step(4 * (PH - 1) + b, b, b < NB - 1)

        @block.scalar
        def _(act):
            def stage_h(v, b):
                held(act, "act", s_ufree, 16 * v + R)
                act.copy(hp[:, :], h[:, b, :]).then_inc(s_h, 1)

            def exponents(v, p):
                held(act, "act", s_best, v + 1)
                act.activation(e[p][:, :], best[p][:, :], ACT.Exp, bias=negm[p][:, 0:1],
                               accum_out=esum[p][:, 0:1]).then_inc(s_exp, 1)

            def take_queries(t, c):
                held(act, "act", s_q, t + 1)
                act.copy(qT[c][:, :], bankA[:, :]).then_inc(s_qT, 1)

            def weights(v, p):
                held(act, "act", s_ufree, 16 * v + 16 + R)
                act.activation(ga[p][:, :], a[p][:, :], ACT.Gelu).then_inc(s_gelu, 1)
                held(act, "act", s_dgfree, v + 1)
                held(act, "act", s_w, v + 1)
                for k in range(TOPK):
                    act.activation(diag[p][:, k, :], ident[:, :], ACT.Copy, scale=w[p][:, k:k + 1]).then_inc(s_dg, 1)

            def step(hd, b, last):
                v, p = 4 * hd + b, b % 2
                if not (last and b == NB - 1):
                    stage_h(v + 1, (b + 1) % NB)
                if not (last and b >= NB - 2):
                    exponents(v + 2, p)
                if b < 2 and not last:
                    take_queries(2 * hd + 2 + b, b)
                if not (last and b == NB - 1):
                    weights(v + 1, 1 - p)

            norm_act(act, N)
            for c in range(2):
                take_queries(c, c)
            stage_h(0, 0)
            exponents(0, 0)
            exponents(1, 1)
            weights(0, 0)
            with act.Fori(0, PH - 1) as hd:
                for b in range(NB):
                    step(hd, b, False)
            for b in range(NB):
                step(PH - 1, b, True)

        @block.vector
        def _(dve):
            ch = Chain(dve, s_chain)

            def both(f):
                for c in range(2):
                    f(c).then_inc(s_chain, 1)
                ch.n += 2
                dve.wait_ge(s_chain, ch.n)

            def take_scores(head):
                held(dve, "dve", s_sd, 2 * head + 2)
                for c, bank in enumerate((bankB, bankA)):
                    dve.tensor_copy(S[:, :, c, :], bank[:, :].rearrange("p (b k) -> p b k", b=NB)).then_inc(s_S, 1)
                held(dve, "dve", s_S, 2 * head + 2)

            def route(p, b):
                s = S[:, b, :, :]
                both(lambda c: dve.max(tops[:, c, 0:8], s[:, c, :]))
                both(lambda c: dve.max_index(topi[:, c, 0:8], tops[:, c, 0:8], s[:, c, :]))
                both(lambda c: dve.match_replace(sc2[:, c, :], tops[:, c, 0:8], s[:, c, :], -3.0e38))
                both(lambda c: dve.max(tops[:, c, 8:16], sc2[:, c, :]))
                both(lambda c: dve.max_index(topi[:, c, 8:16], tops[:, c, 8:16], sc2[:, c, :]))
                dve.tensor_copy(topf[:, :, :], topi[:, :, :]).then_inc(s_chain, 1)
                ch.n += 1
                ch.link(dve.tensor_tensor(cand[:, :, :], bc(tops[:, 0, :].unsqueeze(2), [P, TOPK, TOPK]),
                                          bc(tops[:, 1, :].unsqueeze(1), [P, TOPK, TOPK]), ALU.add))
                c1 = cand[:, :, :].rearrange("p a b -> p (a b)")
                c2 = cand2[:, :, :].rearrange("p a b -> p (a b)")
                ch.link(dve.max(best[p][:, 0:8], c1))
                ch.link(dve.max_index(bestc[:, 0:8], best[p][:, 0:8], c1))
                ch.link(dve.match_replace(c2, best[p][:, 0:8], c1, -3.0e38))
                ch.link(dve.max(best[p][:, 8:16], c2))
                ch.link(dve.max_index(bestc[:, 8:16], best[p][:, 8:16], c2))
                ch.link(dve.tensor_scalar(negm[p][:, :], best[p][:, 0:1], -1.0, None, ALU.mult))
                dve.sem_inc(s_best, 1)
                ch.link(dve.tensor_scalar(ab[:, 0, :], bestc[:, :], 4, None, ALU.logical_shift_right))
                ch.link(dve.tensor_scalar(ab[:, 1, :], bestc[:, :], 15, None, ALU.bitwise_and))
                ch.link(dve.tensor_copy(abf[:, :, :], ab[:, :, :]))
                ch.link(dve.tensor_tensor(hit[:, :, :, :], bc(abf[:, :, :].unsqueeze(3), [P, 2, TOPK, TOPK]),
                                          bc(iota[:, :].unsqueeze(1).unsqueeze(1), [P, 2, TOPK, TOPK]), ALU.is_equal))
                ch.link(dve.tensor_tensor(hit[:, :, :, :], hit[:, :, :, :],
                                          bc(topf[:, :, :].unsqueeze(2), [P, 2, TOPK, TOPK]), ALU.mult))
                ch.link(dve.tensor_reduce(sel[:, :, :], hit[:, :, :, :], AX_X, ALU.add))
                ch.link(dve.scalar_tensor_tensor(flat[:, :], sel[:, 0, :], float(PK), sel[:, 1, :], ALU.mult, ALU.add))
                ch.link(dve.tensor_scalar(idu[p][:, :], flat[:, :], float(layer * NEXP), None, ALU.add))
                dve.sem_inc(s_idu, 1)

            def v_indices(p):
                ch.link(dve.tensor_copy(idv[p][:, :], idu[p][:, :]))
                dve.sem_inc(s_idv, 1)

            def dots(v, p):
                held(dve, "dve", s_h, v + 1)
                for k in range(TOPK):
                    dve.wait_ge(s_ug[k % R], 32 * v + 16 * (k // R + 1))
                    dve.tensor_tensor_reduce(urow[:, k % R, :], urow[:, k % R, :], hp[:, :], 1.0, 0.0,
                                             ALU.mult, ALU.add, a[p][:, k:k + 1]).then_inc(s_ufree, 1)
                held(dve, "dve", s_exp, v + 1)
                ch.link(dve.reciprocal(rs[p][:, :], esum[p][:, :]))
                held(dve, "dve", s_gelu, v + 1)
                ch.link(dve.scalar_tensor_tensor(w[p][:, :], ga[p][:, :], rs[p][:, 0:1], e[p][:, :],
                                                 ALU.mult, ALU.mult))
                dve.sem_inc(s_w, 1)

            def step(hd, b, last):
                v, p = 4 * hd + b, b % 2
                dve.sem_clear(s_chain)
                ch.n = 0
                if not (last and b == NB - 1):
                    v_indices(1 - p)
                if b == 2 and not last:
                    take_scores(hd + 1)
                if not (last and b >= NB - 2):
                    route(p, (b + 2) % NB)
                if not (last and b == NB - 1):
                    dots(v + 1, 1 - p)
                held(dve, "dve", s_acc, v + 1)
                ch.link(dve.tensor_tensor(x[:, b, :], x[:, b, :], acc[p][:, :], ALU.add))
                dve.sem_inc(s_accfree, 1)

            dve.sem_inc(s_ufree, R)
            dve.sem_inc(s_accfree, 2)
            norm_dve(dve, N)
            take_scores(0)
            route(0, 0)
            route(1, 1)
            v_indices(0)
            dots(0, 0)
            with dve.Fori(0, PH - 1) as hd:
                for b in range(NB):
                    step(hd, b, False)
            for b in range(NB):
                step(PH - 1, b, True)

        @block.tensor
        def _(pe):
            def queries(head, c, first=False):
                pe.wait_ge(s_wq[c], 16 * (head + 1))
                if c == 1:
                    pe.wait_ge(s_qT, 2 * head + 1)
                elif not first:
                    pe.wait_ge(s_S, 2 * head)
                for k in range(KD):
                    mm = pe.matmul(bankA[:, :], wq[c][:, k, :], hT[:, k, :], start=(k == 0), stop=(k == KD - 1))
                mm.then_inc(s_q, 1)

            def scores(head, c):
                pe.wait_ge(s_keys[c], 16 * (head + 1))
                pe.wait_ge(s_qT, 2 * head + c + 1)
                for b in range(NB):
                    mm = pe.matmul((bankB, bankA)[c][:, b * PK:(b + 1) * PK], qT[c][:, b * P:(b + 1) * P],
                                   keys[c][:, :], start=True, stop=True, skip_group_check=True)
                mm.then_inc(s_sd, 1)

            def release(head, c):
                pe.wait_ge(s_sd, 2 * head + c + 1)
                pe.sem_inc(s_wqfree, 1)

            def step(hd, b, last):
                v, p = 4 * hd + b, b % 2
                if b == 0 and not last:
                    queries(hd + 1, 0)
                if b == 1 and not last:
                    scores(hd + 1, 0)
                    queries(hd + 1, 1)
                pe.wait_ge(s_accfree, v + 1)
                for k in range(TOPK):
                    if k == TOPK // 2 and b == 1 and not last:
                        scores(hd + 1, 1)
                    pe.wait_ge(s_dg, 16 * v + k + 1)
                    pe.wait_ge(s_vg[k % R], 32 * v + 16 * (k // R + 1))
                    for half in range(2):
                        mm = pe.matmul(acc[p][:, half * 512:(half + 1) * 512], diag[p][:, k, :],
                                       vrow[:, k % R, half * 512:(half + 1) * 512],
                                       start=(k == 0), stop=(k == TOPK - 1))
                    mm.then_inc(s_vfree, 1)
                pe.wait_ge(s_vfree, 16 * v + 16 + R)
                pe.sem_inc(s_acc, 1)
                pe.sem_inc(s_dgfree, 1)
                if b == 1 and not last:
                    for c in range(2):
                        release(hd + 1, c)

            norm_pe(pe, N)
            pe.wait_ge(N.hT_ready, 2 * NB)
            queries(0, 0, True)
            scores(0, 0)
            queries(0, 1)
            scores(0, 1)
            for c in range(2):
                release(0, c)
            pe.sem_inc(s_vfree, R)
            pe.sem_inc(s_dgfree, 2)
            with pe.Fori(0, PH - 1) as hd:
                for b in range(NB):
                    step(hd, b, False)
            for b in range(NB):
                step(PH - 1, b, True)



def attention_mixer(nc, D, x, ident, loaded):
    QUADS = NB * NH // 4
    SLOT = (0, 2, 1, 3)
    with ExitStack() as ctx:
        def sb(name, shape, dt=F32):
            return ctx.enter_context(nc.sbuf_tensor("at_" + name, shape, dt))

        sem = Sems(nc, ctx, "at_")

        h = sb("h", [P, NB, DM])
        hT = sb("hT", [P, KD, SEQ])
        g = sb("g", [P, DM])
        stat = sb("stat", [P, 16])
        wqkv = sb("wqkv", [P, KD, QKV])
        wo = sb("wo", [P, KD, DM])
        bias = sb("bias", [P, QKV])
        cs = sb("cos_sin", [P, 2, NB, ROT])
        sinks = sb("sinks", [P, NH])
        mask = sb("mask", [P, 2, 2 * P])
        qk = sb("qk", [P, NB, NH + NKV, HD])
        kd = sb("kd", [P, NB, NKV, 2, HD])
        v = sb("v", [P, NB + 1, NKV * HD])
        rt = sb("rope_tmp", [P, 4, NH + NKV, ROT])
        qT = sb("qT", [P, NB, KD, P])
        kT = sb("kT", [P, NKV, P + SEQ])
        sc, pe_ = sb("scores", [P, 2, 4, 2 * P]), sb("probs", [P, 2, 4, 2 * P])
        pT = sb("probsT", [P, 2, 8, P])
        sm = sb("softmax_cols", [P, 2, 8, 4])
        bank = [ctx.enter_context(nc.psum_tensor(f"at_ps{i}", [P, 2, 512], F32)) for i in range(4)]

        def B(i):
            return bank[i // 2][:, i % 2, :]

        tp = [B(6).rearrange("p (a b) -> p a b", a=4), B(7).rearrange("p (a b) -> p a b", a=4)]
        s_w, s_wo, s_c = sem("wqkv_loaded"), sem("wo_loaded"), sem("constants_loaded")
        s_pad = sem("padding_zeroed")
        s_p, s_pt = sem("qkv_piece_done"), sem("qkv_piece_taken")
        s_chain = sem("dve_chain")
        s_rope = sem("block_rotated")
        s_tq, s_tqt = sem("qk_turned"), sem("qk_turned_taken")
        s_s, s_sm, s_nm = sem("scores_done"), sem("scores_masked"), sem("maximum_ready")
        s_e, s_pn = sem("exponents_ready"), sem("probs_ready")
        s_tpd, s_tpt = sem("probs_turned"), sem("probs_turned_taken")
        s_pv, s_pvt = sem("pv_done"), sem("pv_taken")
        s_o, s_xr = sem("out_block_done"), sem("residual_added")
        N = Norm(sem, "n", x, h, hT, stat, g, tp, ident[:, :])
        N.x_loaded, N.x_loaded_at = loaded, 32
        N.ident_loaded, N.ident_loaded_at = loaded, 32
        PIECES = [(0, 512), (512, 512), (1024, 256)]
        block = sem.block()

        @block.sync
        def _(sp):
            sp.dma_start(g[:, :], D["g_mix"][1:2, :].to_broadcast([P, DM])).then_inc(N.g_loaded, 16)
            sp.dma_start(wqkv[:, :, :], D["w_qkv"].rearrange("(k p) c -> p k c", p=P)).then_inc(s_w, 16)
            sp.dma_start(bias[:, :], D["b_qkv"].to_broadcast([P, QKV])).then_inc(s_c, 16)
            sp.dma_start(cs[:, :, :, :], D["rope"]).then_inc(s_c, 16)
            sp.dma_start(sinks[:, :], D["sinks"].to_broadcast([P, NH])).then_inc(s_c, 16)
            sp.dma_start(mask[:, :, :], D["masks"]).then_inc(s_c, 16)
            sp.dma_start(wo[:, :, :], D["w_o"].rearrange("(k p) c -> p k c", p=P)).then_inc(s_wo, 16)

        @block.gpsimd
        def _(pool):
            pool.memset(kT[:, :, 0:P], 0.0).then_inc(s_pad, 1)
            pool.memset(v[:, 0, :], 0.0).then_inc(s_pad, 1)

        @block.scalar
        def _(act):
            norm_act(act, N)
            for b in range(NB):
                for q in range(2):
                    act.wait_ge(s_tq, 3 * b + q + 1)
                    act.copy(qT[:, b, 4 * q:4 * q + 4, :].rearrange("p a t -> p (a t)"), B(4 + q)).then_inc(s_tqt, 1)
                act.wait_ge(s_tq, 3 * b + 3)
                act.copy(kT[:, :, P + b * P:P + (b + 1) * P],
                         B(6)[:, 0:2 * P].rearrange("p (g t) -> p g t", g=2)).then_inc(s_tqt, 1)

            def exps(n):
                act.wait_ge(s_nm, n + 1)
                if n >= 2:
                    act.wait_ge(s_tpd, n - 1)
                for j in range(4):
                    act.activation(pe_[:, n % 2, j, :], sc[:, n % 2, j, :], ACT.Exp, bias=sm[:, n % 2, 2, j:j + 1],
                                   accum_out=sm[:, n % 2, 5, j:j + 1]).then_inc(s_e, 1)
                act.activation(sm[:, n % 2, 4, :], sm[:, n % 2, 3, :], ACT.Exp).then_inc(s_e, 1)

            exps(0)
            for n in range(QUADS):
                if n + 1 < QUADS:
                    exps(n + 1)
                act.wait_ge(s_tpd, n + 1)
                if n >= 2:
                    act.wait_ge(s_pv, n - 1)
                act.copy(pT[:, n % 2, :, :].rearrange("p (a c) t -> p a (c t)", a=2), bank[2][:, :, :]).then_inc(s_tpt, 1)
                act.wait_ge(s_pv, n + 1)
                b, quad = n // 4, n % 4
                act.copy(hT[:, 2 * quad:2 * quad + 2, b * P:(b + 1) * P],
                         B(6 + n % 2)[:, 0:2 * P].rearrange("p (m t) -> p m t", m=2)).then_inc(s_pvt, 1)

        @block.vector
        def _(dve):
            norm_dve(dve, N)
            ch = Chain(dve, s_chain)
            dve.wait_ge(s_c, 64)
            for b in range(NB):
                for q, (c0, cn) in enumerate(PIECES):
                    m = 3 * b + q
                    dve.wait_ge(s_p, m + 1)
                    ps = B(m % 4)
                    if q < 2:
                        dve.tensor_tensor(qk[:, b, 8 * q:8 * q + 8, :].rearrange("p n d -> p (n d)"), ps,
                                          bias[:, c0:c0 + cn], ALU.add).then_inc(s_pt, 1)
                    else:
                        dve.tensor_tensor(qk[:, b, NH:, :].rearrange("p n d -> p (n d)"), ps[:, 0:P],
                                          bias[:, c0:c0 + P], ALU.add).then_inc(s_chain, 1)
                        ch.n += 1
                        dve.tensor_tensor(v[:, b + 1, :], ps[:, P:2 * P], bias[:, c0 + P:c0 + 2 * P],
                                          ALU.add).then_inc(s_pt, 1)
                dve.wait_ge(s_pt, 3 * b + 3)
                dve.wait_ge(s_chain, ch.n)
                x1, x2 = qk[:, b, :, 0:ROT], qk[:, b, :, ROT:2 * ROT]
                co = bc(cs[:, 0, b, :].unsqueeze(1), [P, NH + NKV, ROT])
                si = bc(cs[:, 1, b, :].unsqueeze(1), [P, NH + NKV, ROT])
                for t, (u, w) in enumerate(((x1, co), (x2, si), (x2, co), (x1, si))):
                    dve.tensor_tensor(rt[:, t, :, :], u, w, ALU.mult).then_inc(s_chain, 1)
                ch.n += 4
                dve.wait_ge(s_chain, ch.n)
                dve.tensor_tensor(x1, rt[:, 0, :, :], rt[:, 1, :, :], ALU.subtract).then_inc(s_chain, 1)
                dve.tensor_tensor(x2, rt[:, 2, :, :], rt[:, 3, :, :], ALU.add).then_inc(s_chain, 1)
                ch.n += 2
                dve.wait_ge(s_chain, ch.n)
                dve.tensor_copy(kd[:, b, :, :, :], bc(qk[:, b, NH:, :].unsqueeze(2), [P, NKV, 2, HD])).then_inc(s_rope, 1)

            def front(n):
                b, quad = n // 4, n % 4
                dve.wait_ge(s_s, n + 1)
                if n >= 2:
                    dve.wait_ge(s_e, 5 * (n - 1))
                dve.scalar_tensor_tensor(sc[:, n % 2, :, :], bank[n % 2][:, :, :].rearrange("p a (c k) -> p (a c) k", c=2),
                                         HD ** -0.5, bc(mask[:, min(b, 1), :].unsqueeze(1), [P, 4, 2 * P]),
                                         ALU.mult, ALU.add).then_inc(s_sm, 1)
                dve.wait_ge(s_sm, n + 1)
                c = sm[:, n % 2, :, :]
                sk = sinks[:, 4 * quad:4 * quad + 4]
                ch.link(dve.tensor_reduce(c[:, 0, :], sc[:, n % 2, :, :], AX_X, ALU.max))
                ch.link(dve.tensor_tensor(c[:, 1, :], c[:, 0, :], sk, ALU.max))
                ch.link(dve.tensor_tensor(c[:, 3, :], sk, c[:, 1, :], ALU.subtract))
                dve.tensor_scalar(c[:, 2, :], c[:, 1, :], -1.0, None, ALU.mult).then_inc(s_nm, 1)

            def back(n):
                dve.wait_ge(s_e, 5 * (n + 1))
                c = sm[:, n % 2, :, :]
                ch.link(dve.tensor_tensor(c[:, 6, :], c[:, 5, :], c[:, 4, :], ALU.add))
                ch.link(dve.reciprocal(c[:, 7, :], c[:, 6, :]))
                dve.tensor_tensor(pe_[:, n % 2, :, :], pe_[:, n % 2, :, :],
                                  bc(c[:, 7, :].unsqueeze(2), [P, 4, 2 * P]), ALU.mult).then_inc(s_pn, 1)

            front(0)
            for n in range(QUADS):
                if n + 1 < QUADS:
                    front(n + 1)
                back(n)
            for n in range(2 * NB):
                dve.wait_ge(s_o, n + 1)
                b, half = n // 2, n % 2
                xs = x[:, b, half * 512:(half + 1) * 512]
                dve.tensor_tensor(xs, xs, B(n), ALU.add).then_inc(s_xr, 1)
            dve.wait_ge(s_xr, 2 * NB)

        @block.tensor
        def _(pe):
            norm_pe(pe, N)
            pe.wait_ge(N.hT_ready, 2 * NB)
            pe.wait_ge(s_w, 16)

            def project(b):
                for q, (c0, cn) in enumerate(PIECES):
                    m = 3 * b + q
                    if m >= 4:
                        pe.wait_ge(s_pt, m - 3)
                    for k in range(KD):
                        mm = pe.matmul(B(m % 4)[:, 0:cn], hT[:, k, b * P:(b + 1) * P], wqkv[:, k, c0:c0 + cn],
                                       start=(k == 0), stop=(k == KD - 1))
                    mm.then_inc(s_p, 1)

            def turn(b):
                pe.wait_ge(s_rope, b + 1)
                if b:
                    pe.wait_ge(s_tqt, 3 * b)
                for q in range(2):
                    for t in range(4):
                        m = 4 * q + t
                        mm = pe.transpose(B(4 + q)[:, t * P:(t + 1) * P],
                                          qk[:, b, 2 * m:2 * m + 2, :].rearrange("p n d -> p (n d)"), ident[:, :])
                    mm.then_inc(s_tq, 1)
                for t in range(NKV):
                    mm = pe.transpose(B(6)[:, t * P:(t + 1) * P], kd[:, b, t, :, :].rearrange("p n d -> p (n d)"),
                                      ident[:, :])
                mm.then_inc(s_tq, 1)

            project(0)
            for b in range(NB):
                if b + 1 < NB:
                    project(b + 1)
                turn(b)

            def scores(n):
                b, quad = n // 4, n % 4
                if n == 0:
                    pe.wait_ge(s_pt, 3 * NB)
                if n % 4 == 0:
                    pe.wait_ge(s_tqt, 3 * NB if n == 0 else 3 * NB)
                if n >= 2:
                    pe.wait_ge(s_sm, n - 1)
                for j in range(4):
                    hq = 4 * quad + j
                    r, grp = 64 * (hq % 2), hq // (NH // NKV)
                    mm = pe.matmul(bank[n % 2][:, j % 2, (j // 2) * 2 * P:(j // 2 + 1) * 2 * P],
                                   qT[r:r + 64, b, hq // 2, :], kT[r:r + 64, grp, b * P:(b + 2) * P],
                                   start=True, stop=True, skip_group_check=True, tile_position=(r, 0))
                mm.then_inc(s_s, 1)

            pe.wait_ge(s_pad, 2)
            scores(0)
            scores(1)
            for n in range(QUADS):
                b, quad = n // 4, n % 4
                pe.wait_ge(s_pn, n + 1)
                if n:
                    pe.wait_ge(s_tpt, n)
                for t in range(8):
                    mm = pe.transpose(bank[2][:, t // 4, (t % 4) * P:(t % 4 + 1) * P],
                                      pe_[:, n % 2, t // 2, (t % 2) * P:(t % 2 + 1) * P], ident[:, :])
                mm.then_inc(s_tpd, 1)
                if n + 2 < QUADS:
                    scores(n + 2)
                pe.wait_ge(s_tpt, n + 1)
                if n >= 2:
                    pe.wait_ge(s_pvt, n - 1)
                for j in range(4):
                    hq = 4 * quad + j
                    r, grp = 64 * (hq % 2), hq // (NH // NKV)
                    for side in range(2):
                        mm = pe.matmul(B(6 + n % 2)[r:r + 64, (j // 2) * P:(j // 2 + 1) * P],
                                       v[:, b + side, grp * HD:(grp + 1) * HD], pT[:, n % 2, 2 * SLOT[j] + side, :],
                                       start=(side == 0), stop=(side == 1), tile_position=(0, r))
                mm.then_inc(s_pv, 1)
            pe.wait_ge(s_pvt, QUADS)
            pe.wait_ge(s_wo, 16)
            for o in range(2 * NB):
                b, half = o // 2, o % 2
                for k in range(KD):
                    mm = pe.matmul(B(o), hT[:, k, b * P:(b + 1) * P], wo[:, k, half * 512:(half + 1) * 512],
                                   start=(k == 0), stop=(k == KD - 1))
                mm.then_inc(s_o, 1)


def final_norm(nc, D, x, loaded, out):
    with ExitStack() as ctx:
        sem = Sems(nc, ctx, "f_")

        h = ctx.enter_context(nc.sbuf_tensor("f_h", [P, NB, DM], F32))
        g = ctx.enter_context(nc.sbuf_tensor("f_g", [P, DM], F32))
        stat = ctx.enter_context(nc.sbuf_tensor("f_stat", [P, 16], F32))
        N = Norm(sem, "n", x, h, None, stat, g, None, None)
        N.x_loaded, N.x_loaded_at = loaded, 32
        s_out = sem("out_stored")
        block = sem.block()

        @block.sync
        def _(sp):
            sp.dma_start(g[:, :], D["g_fin"].to_broadcast([P, DM])).then_inc(N.g_loaded, 16)
            for b in range(NB):
                sp.wait_ge(N.h_ready, b + 1)
                sp.dma_start(out[b * P:(b + 1) * P, :], h[:, b, :]).then_inc(s_out, 16)
            sp.wait_ge(s_out, 16 * NB)

        @block.scalar
        def _(act):
            norm_act(act, N)

        @block.vector
        def _(dve):
            norm_dve(dve, N)


def build(nc, D, out):
    with ExitStack() as ctx:
        x = ctx.enter_context(nc.sbuf_tensor("x_res", [P, NB, DM], F32))
        ident = ctx.enter_context(nc.sbuf_tensor("ident", [P, P], F32))
        loaded = ctx.enter_context(nc.semaphore("x_and_ident_loaded"))
        iota = ctx.enter_context(nc.sbuf_tensor("iota16", [P, TOPK], F32))
        hybrid_mixer(nc, D, x, ident, loaded, iota)
        peer(nc, D, 0, x, ident, loaded, iota)
        attention_mixer(nc, D, x, ident, loaded)
        peer(nc, D, 1, x, ident, loaded, iota)
        final_norm(nc, D, x, loaded, out)


def kernel(**inputs):
    import concourse.bacc as _bacc
    from concourse.bass_utils import run_bass_kernel_spmd as _run
    a = {k: np.asarray(v) for k, v in inputs.items()}
    f = np.float32

    def tiles(v, n):
        return v.reshape(n, P).T

    G2 = (S5_G // 2, 2)
    re, im = a["s5_lambda_re"][0], a["s5_lambda_im"][0]
    step = np.broadcast_to(a["s5_log_step"][0][:, None], (S5_G, S5_P))
    scal = np.stack([tiles(re, NST), tiles(im, NST), tiles(step, NST)], 1)
    bT = np.zeros((2, UT, 4, 2, S5_H, 2, S5_P), f)
    cT = np.zeros((2, NST, 2, S5_P, 2, S5_H), f)
    for part, (bn, cn) in enumerate((("s5_b_re", "s5_c_re"), ("s5_b_im", "s5_c_im"))):
        b = a[bn][0].reshape(UT, 4, 2, S5_P, S5_H)
        c = a[cn][0].reshape(NST, 2, S5_H, S5_P)
        for q in range(2):
            bT[part, :, :, q, :, q, :] = b[:, :, q].transpose(0, 1, 3, 2)
            cT[part, :, q, :, q, :] = c[:, q].transpose(0, 2, 1)
    bT = bT.reshape(2, UT, P, P).transpose(2, 0, 1, 3)
    cT = cT.reshape(2, NST, P, 32).transpose(2, 0, 1, 3)
    cols = np.stack([tiles(a[n][0].reshape(-1), UT) for n in ("s5_d", "conv_dw_b", "conv_ln_g", "conv_ln_b")], 1)
    conv_w = a["conv_dw_w"][0].T.reshape(UT, P, CONV_K).transpose(1, 0, 2)

    keysT = a["peer_sub_keys"].reshape(2, NQT, PK, P).transpose(0, 1, 3, 2)
    w_q = a["peer_w_q"].reshape(2, KD, P, NQT, P).transpose(0, 3, 2, 1, 4).reshape(2, NQT, P, DM)
    inv = np.power(f(500000.0), -np.arange(0, 2 * ROT, 2, dtype=f) / f(2 * ROT)).astype(f)
    ang = np.arange(SEQ, dtype=f)[:, None] * inv[None, :]
    rope = np.stack([np.cos(ang), np.sin(ang)]).astype(f).reshape(2, NB, P, ROT).transpose(2, 0, 1, 3)
    diff = P + np.arange(P)[:, None] - np.arange(2 * P)[None, :]
    band = (diff >= 0) & (diff < P)
    masks = np.stack([np.where(band & (np.arange(2 * P) >= P), 0.0, NEG), np.where(band, 0.0, NEG)], 1).astype(f)
    D = {"w_qkv": a["attn_w_qkv"][0], "b_qkv": a["attn_b_qkv"], "sinks": a["attn_sinks"].reshape(NH // 4, 2, 2).transpose(0, 2, 1).reshape(1, NH), "w_o": a["attn_w_o"][0],
         "rope": rope, "masks": masks, "g_fin": a["norm_final"][None],
         "keysT": keysT, "w_q": w_q, "g_ffn": a["norm_ffn"], "peer_u": a["peer_u"], "peer_v": a["peer_v"],
         "x": a["x"][0], "ident": np.eye(P, dtype=f), "g_mix": a["norm_mix"],
         "s5_scal": scal, "s5_bT": bT, "s5_cT": cT, "chan_cols": cols, "conv_w": conv_w,
         "w_in": a["mix_w_in"][0], "w_glu": a["s5_w_glu"][0], "w_out": a["mix_w_out"][0]}

    nc = _bacc.Bacc("TRN2", target_bir_lowering=False, num_devices=1)
    arrays, aps = {}, {}
    for name, v in D.items():
        v = np.ascontiguousarray(v)
        arrays[f"in_{name}"] = v
        aps[name] = nc.dram_tensor(f"in_{name}", v.shape, mybir.dt.from_np(v.dtype), kind="ExternalInput").ap()
    out = nc.dram_tensor("out", (SEQ, DM), F32, kind="ExternalOutput").ap()
    build(nc, aps, out)
    r = _run(nc, [arrays], core_ids=[0])
    return r.results[0]["out"].reshape(1, SEQ, DM)
```

```python
import concourse.bass as bass
from concourse import mybir
from concourse.alu_op_type import AluOpType
from contextlib import ExitStack
import math
import numpy as np

P = 128
F32 = mybir.dt.float32
I32 = mybir.dt.int32
U32 = mybir.dt.uint32
F32R = mybir.dt.float32r
ALU = AluOpType
ACT = mybir.ActivationFunctionType
AX_X = mybir.AxisListType.X

SEQ, DM = 512, 1024
NB = SEQ // P
KD = DM // P
EPS = 1e-6
S5_W, S5_G, S5_H, S5_P = 512, 32, 16, 64
NST = S5_G * S5_P // P
UT = S5_W // P
CONV_K = 31
NH, NKV, HD, ROT = 16, 2, 64, 8
QKV = (NH + 2 * NKV) * HD
NEG = -1.0e30
PH, PK, TOPK = 8, 128, 16
NEXP = PK * PK
NQT = 2 * PH


class Chain:

    def __init__(self, eng, sem):
        self.eng, self.sem, self.n = eng, sem, 0

    def link(self, ins):
        self.n += 1
        ins.then_inc(self.sem, 1)
        self.eng.wait_ge(self.sem, self.n)


class Sems:

    def __init__(self, nc, ctx, tag):
        self.nc, self.ctx, self.tag, self.made = nc, ctx, tag, []

    def __call__(self, name):
        s = self.nc.alloc_semaphore(self.tag + name)
        self.made.append(s)
        return s

    def block(self):
        self.ctx.callback(self.clear)
        return self.ctx.enter_context(self.nc.Block())

    def clear(self):
        self.nc.clear_and_free_semaphores(self.made)
        self.nc.all_engine_barrier()


def bc(ap, shape):
    return ap.broadcast_to(shape)




class Norm:

    def __init__(self, sem, tag, x, h, hT, stat, g, tp, ident):
        self.x, self.h, self.hT, self.stat, self.g, self.tp, self.ident = x, h, hT, stat, g, tp, ident
        self.squares, self.mean_ready = sem(tag + "_squares"), sem(tag + "_mean_ready")
        self.root, self.rstd_ready = sem(tag + "_root"), sem(tag + "_rstd_ready")
        self.g_loaded, self.h_ready = sem(tag + "_g_loaded"), sem(tag + "_h_ready")
        self.turned, self.hT_ready = sem(tag + "_turned"), sem(tag + "_hT_ready")

    def act_sums(self, act, b, x_ready, value):
        act.wait_ge(x_ready, value)
        act.activation(self.h[:, b, :], self.x[:, b, :], ACT.Square,
                       accum_out=self.stat[:, 0, b:b + 1]).then_inc(self.squares, 1)
        act.wait_ge(self.mean_ready, b + 1)
        act.activation(self.stat[:, 2, b:b + 1], self.stat[:, 1, b:b + 1], ACT.Sqrt).then_inc(self.root, 1)

    def dve_scale(self, dve, b):
        dve.wait_ge(self.squares, b + 1)
        dve.tensor_scalar(self.stat[:, 1, b:b + 1], self.stat[:, 0, b:b + 1], 1.0 / DM, EPS, ALU.mult, ALU.add)\
           .then_inc(self.mean_ready, 1)
        dve.wait_ge(self.root, b + 1)
        dve.reciprocal(self.stat[:, 3, b:b + 1], self.stat[:, 2, b:b + 1]).then_inc(self.rstd_ready, 1)
        dve.wait_ge(self.rstd_ready, b + 1)
        if b == 0:
            dve.wait_ge(self.g_loaded, 16)
        dve.scalar_tensor_tensor(self.h[:, b, :], self.x[:, b, :], self.stat[:, 3, b:b + 1], self.g,
                                 ALU.mult, ALU.mult).then_inc(self.h_ready, 1)

    def pe_turn(self, pe, b):
        pe.wait_ge(self.h_ready, b + 1)
        for n in (2 * b, 2 * b + 1):
            if n >= 2:
                pe.wait_ge(self.hT_ready, n - 1)
            for q in range(4):
                k = 4 * (n % 2) + q
                mm = pe.transpose(self.tp[n % 2][:, q, :], self.h[:, b, k * P:(k + 1) * P], self.ident)
            mm.then_inc(self.turned, 1)

    def act_take(self, act, b):
        for n in (2 * b, 2 * b + 1):
            act.wait_ge(self.turned, n + 1)
            half = n % 2
            act.copy(self.hT[:, 4 * half:4 * half + 4, b * P:(b + 1) * P], self.tp[half]).then_inc(self.hT_ready, 1)

    def act_all(self, act, x_ready, values):
        for b in range(NB):
            self.act_sums(act, b, x_ready, values[b])
            if b:
                self.act_take(act, b - 1)
        self.act_take(act, NB - 1)


def first_queries(sp, D, layer, wq, used, value, landed):
    sp.wait_ge(used, value)
    sp.dma_start(wq[:, :, :], D["w_q"][layer, 0:2].rearrange("c p w -> p c w")).then_inc(landed, 16)



def hybrid_mixer(nc, D, x, h, hT, wq, low, stat, ident, loaded, iota):
    with ExitStack() as ctx:
        def sb(name, shape, dt=F32):
            return ctx.enter_context(nc.sbuf_tensor(name, shape, dt))

        sem = Sems(nc, ctx, "m0_")

        late = h[:, :, :].rearrange("p b (two t) -> p (b two) t", two=2)
        yg, cv = late[:, 0:4, :], late[:, 4:8, :]
        PAD = CONV_K - 1
        vpad_lo, diag_lo = low
        wring = sb("m0_wring", [P, 4, 1024])
        uT = wq[:, :, :].rearrange("p c (two t) -> p (c two) t", two=2)
        vpad = [sb("m0_vpad", [P, UT, PAD + SEQ], F32R), vpad_lo]
        gsg = sb("m0_gsg", [P, 2, SEQ])
        g = gsg[:, :, :].rearrange("p a t -> p (a t)")
        ec = sb("m0_ec", [P, NST, SEQ])
        w_out = ec[:, :, :].rearrange("p (k two) t -> p k (two t)", two=2)
        es = sb("m0_es", [P, NST, SEQ])
        work = sb("m0_work", [P, 16, SEQ])
        tmp_c = work[:, 0:4, :].rearrange("p a t -> p (a t)")
        tmp_s = work[:, 4:8, :].rearrange("p a t -> p (a t)")
        rot = work[:, 0:4, :]
        st = work[:, 4:8, :].rearrange("p (b r) t -> p b r t", b=2)
        pr = work[:, 8:16, :].rearrange("p (b r) t -> p b r t", b=2)
        diag = [sb("m0_diag", [P, 8, P], F32R), diag_lo]
        bT = sb("m0_bT", [P, 2, UT, P])
        cT = sb("m0_cT", [P, 2, NST, 32])
        cc = sb("m0_cc", [P, 3, NST, 32])
        sp = sb("m0_sp", [P, 3, NST])
        pv = sb("m0_pv", [P, 40, NST])
        pw = sb("m0_pw", [P, 2, 9, NST])
        dcol = sb("m0_dcol", [P, 4, UT])
        cw = sb("m0_cw", [P, UT, CONV_K])
        cw_hi, cw_lo = sb("m0_cw_hi", [P, UT, CONV_K], F32R), sb("m0_cw_lo", [P, UT, CONV_K])
        ones = sb("m0_ones", [P, P])

        bank = [ctx.enter_context(nc.psum_tensor(f"m0_ps{i}", [P, SEQ], F32)) for i in range(8)]
        tp = [bank[6][:, :].rearrange("p (a b) -> p a b", a=4), bank[7][:, :].rearrange("p (a b) -> p a b", a=4)]

        s_par = sem("params_loaded")
        s_win = [sem(f"weight_tile{i}_loaded") for i in range(4)]
        s_wuse = sem("weight_tiles_used")
        s_chain = sem("dve_chain")
        s_sin_in = sem("angle_reduced")
        s_sin = sem("sines_ready")
        s_pow = sem("powers_ready")
        s_first = sem("tables_started")
        s_ec, s_es = sem("cos_table_level"), sem("sin_table_level")
        s_poolc = sem("pool_chain")
        s_coef = sem("c_scaled")
        s_z = sem("z_tile_done")
        s_zact, s_zdve = sem("z_tile_taken_by_act"), sem("z_tile_taken_by_dve")
        s_pad = sem("pad_zeroed")
        s_v = sem("input_products_ready")
        s_vused = sem("input_products_taken")
        s_state = sem("states_scanned")
        s_pd, s_pp = sem("products_by_dve"), sem("products_by_pool")
        s_h = sem("states_rotated")
        s_vlo, s_cw = sem("conv_input_split"), sem("taps_split")
        s_cmm = sem("state_tile_projected")
        s_yd, s_yg = sem("y_with_skip_ready"), sem("y_gelu_ready")
        s_diag = sem("tap_diagonal_ready")
        s_tap = sem("tap_done")
        s_cv = sem("conv_tile_taken")
        s_ones = sem("ones_ready")
        s_mean, s_cen, s_sq = sem("mean_ready"), sem("centred_ready"), sem("centred_squared")
        s_var, s_vr, s_sd = sem("var_ready"), sem("var_eps_ready"), sem("std_ready")
        s_rs, s_yn = sem("rstd_ready"), sem("ln_scaled")
        s_lnout = sem("conv_branch_ready")
        s_glu, s_gs, s_sout = sem("glu_done"), sem("glu_sigmoid_ready"), sem("s5_branch_ready")
        s_o, s_xr = sem("out_block_done"), sem("residual_added")
        s_iota = sem("iota_ready")
        s_x = [sem(f"x{b}_loaded") for b in range(NB)]
        s_wout, s_wq = sem("w_out_loaded"), sem("first_query_weights_loaded")
        N = Norm(sem, "n", x, h, hT, stat, g, tp, ident[:, :])
        tp2 = [bank[i][:, :].rearrange("p (a b) -> p a b", a=4) for i in range(2)]
        N2 = Norm(sem, "n2", x, h, hT, stat, g, tp2, ident[:, :])

        NZ = 12
        zcol = [0, 1, 2, 3] + [c for i in range(UT) for c in (8 + i, 4 + i)]
        win = D["w_in"].rearrange("(k p) (n c) -> n p k c", p=P, c=P)
        wglu = D["w_glu"].rearrange("(k p) c -> p k c", p=P)

        block = sem.block()

        def skip(dve, c):
            dve.wait_ge(s_cmm, 4 * (c + 1))
            dve.scalar_tensor_tensor(yg[:, c, :], uT[:, c, :], dcol[:, 0, c:c + 1], bank[4 + c % 2][:, :],
                                     ALU.mult, ALU.add).then_inc(s_yd, 1)

        @block.sync
        def _(sp_):
            for b in range(NB):
                sp_.dma_start(x[:, b, :], D["x"][b * P:(b + 1) * P, :]).then_inc(s_x[b], 16)
            sp_.dma_start(ident[:, :], D["ident"]).then_inc(loaded, 16)
            sp_.dma_start(g, D["g_mix"][0:1, :].to_broadcast([P, DM])).then_inc(N.g_loaded, 16)
            for dst, src in ((sp[:, :, :], D["s5_scal"]), (bT[:, :, :, :], D["s5_bT"]), (cT[:, :, :, :], D["s5_cT"]),
                             (dcol[:, :, :], D["chan_cols"]), (cw[:, :, :], D["conv_w"])):
                sp_.dma_start(dst, src).then_inc(s_par, 16)
            for n in range(NZ + 2):
                if n >= 4:
                    sp_.wait_ge(s_wuse, n - 3)
                slot = wring[:, n % 4, :]
                if n < NZ:
                    dst, src = slot.rearrange("p (k c) -> p k c", k=KD), win[zcol[n]]
                else:
                    dst, src = slot.rearrange("p (k c) -> p k c", k=2), wglu[:, 2 * (n - NZ):2 * (n - NZ) + 2, :]
                sp_.dma_start(dst, src).then_inc(s_win[n % 4], 16)
            sp_.wait_ge(s_pd, 2 * NST)
            sp_.dma_start(w_out, D["w_out"].rearrange("(k p) c -> p k c", p=P)).then_inc(s_wout, 16)
            first_queries(sp_, D, 0, wq, s_yd, UT, s_wq)
            sp_.wait_ge(s_sout, UT)
            sp_.dma_start(g, D["g_ffn"][0:1, :].to_broadcast([P, DM])).then_inc(N2.g_loaded, 16)
            sp_.wait_ge(s_wq, 16)

        @block.gpsimd
        def _(pool):
            pool.memset(ones[:, :], 1.0 / S5_W).then_inc(s_ones, 1)
            pool.iota(iota[:, :], pattern=[[1, TOPK]], base=0, channel_multiplier=0,
                      allow_small_or_imprecise_dtypes=True).then_inc(s_iota, 1)
            pool.wait_ge(s_iota, 1)
            pool.wait_ge(s_par, 80)
            pool.tensor_copy(cw_hi[:, :, :], cw[:, :, :]).then_inc(s_cw, 1)
            pool.wait_ge(s_cw, 1)
            pool.tensor_tensor(cw_lo[:, :, :], cw[:, :, :], cw_hi[:, :, :], ALU.subtract).then_inc(s_cw, 1)
            pool.wait_ge(s_cw, 2)
            ch = Chain(pool, s_poolc)
            pool.wait_ge(s_pow, 1)
            pool.wait_ge(s_first, 2)
            for j in range(9):
                n = 1 << j
                for a, m in ([(0, n)] if n <= 128 else [(o, 128) for o in range(0, n, 128)]):
                    t = tmp_s[:, 0:NST * m].rearrange("p (k t) -> p k t", k=NST)
                    pc = bc(pw[:, 0, j, :].unsqueeze(2), [P, NST, m])
                    ps = bc(pw[:, 1, j, :].unsqueeze(2), [P, NST, m])
                    pool.wait_ge(s_ec, j)
                    pool.wait_ge(s_es, j)
                    pool.tensor_tensor(es[:, :, n + a:n + a + m], es[:, :, a:a + m], pc, ALU.mult).then_inc(s_poolc, 1)
                    pool.tensor_tensor(t, ec[:, :, a:a + m], ps, ALU.mult).then_inc(s_poolc, 1)
                    ch.n += 2
                    pool.wait_ge(s_poolc, ch.n)
                    ch.link(pool.tensor_tensor(es[:, :, n + a:n + a + m], es[:, :, n + a:n + a + m], t, ALU.add))
                pool.sem_inc(s_es, 1)
            for k in range(NST):
                pool.wait_ge(s_state, 2 * (k + 1))
                if k >= 2:
                    pool.wait_ge(s_cmm, k - 1)
                pool.tensor_tensor(pr[:, k % 2, 1, :], st[:, k % 2, 0, :], es[:, k, :], ALU.mult).then_inc(s_pp, 1)
                pool.tensor_tensor(pr[:, k % 2, 3, :], st[:, k % 2, 1, :], es[:, k, :], ALU.mult).then_inc(s_pp, 1)
                pool.wait_ge(s_pd, 2 * (k + 1))
                pool.wait_ge(s_pp, 2 * (k + 1))
                for o, a, op in ((0, 3, ALU.subtract), (2, 1, ALU.add)):
                    pool.tensor_tensor(pr[:, k % 2, o, :], pr[:, k % 2, o, :], pr[:, k % 2, a, :], op).then_inc(s_h, 1)

        @block.scalar
        def _(act):
            for b in range(NB):
                N.act_sums(act, b, s_x[b], 16)
                if b:
                    N.act_take(act, b - 1)
            N.act_take(act, NB - 1)
            act.wait_ge(s_sin_in, 1)
            act.activation(pv[:, 20, :], pv[:, 15, :], ACT.Sin).then_inc(s_sin, 1)
            act.activation(pv[:, 21, :], pv[:, 15, :], ACT.Sin, scale=0.5).then_inc(s_sin, 1)
            for n in range(UT):
                act.wait_ge(s_z, n + 1)
                act.copy(uT[:, n, :], bank[n % 4][:, :]).then_inc(s_zact, 1)
            for i in range(UT):
                act.wait_ge(s_z, 4 + 2 * i + 1)
                if i >= 2:
                    act.wait_ge(s_zdve, i - 1)
                act.activation(gsg[:, i % 2, :], bank[(4 + 2 * i) % 4][:, :], ACT.Sigmoid).then_inc(s_zact, 1)
            act.wait_ge(s_z, NZ)
            for part in range(2):
                act.activation(vpad[part][:, :, 0:PAD], bc(ident[:, 0:PAD].unsqueeze(1), [P, UT, PAD]), ACT.Copy,
                               scale=0.0).then_inc(s_pad, 1)

            def take_conv(i):
                act.wait_ge(s_tap, CONV_K * (i + 1))
                act.activation(cv[:, i, :], bank[6 + i % 2][:, :], ACT.Identity, bias=dcol[:, 1, i:i + 1])\
                   .then_inc(s_cv, 1)

            def gelu(i):
                act.wait_ge(s_yd, i + 1)
                act.activation(yg[:, i, :], yg[:, i, :], ACT.Gelu).then_inc(s_yg, 1)

            GELU_AT = (74, 102)
            act.wait_ge(s_cw, 2)
            for q in range(UT * CONV_K):
                if q >= 8:
                    act.wait_ge(s_tap, q - 7)
                for part, c in ((0, cw_hi), (1, cw_lo)):
                    act.activation(diag[part][:, q % 8, :], ident[:, :], ACT.Copy,
                                   scale=c[:, q // CONV_K, q % CONV_K:q % CONV_K + 1].bitcast(F32)).then_inc(s_diag, 1)
                if q >= CONV_K and q % CONV_K == 3:
                    take_conv(q // CONV_K - 1)
                if q in GELU_AT:
                    gelu(GELU_AT.index(q))
            take_conv(UT - 1)
            gelu(2)
            gelu(3)
            for i in range(UT):
                act.wait_ge(s_cen, i + 1)
                act.activation(rot[:, i, :], cv[:, i, :], ACT.Square).then_inc(s_sq, 1)
            for i in range(UT):
                act.wait_ge(s_glu, i + 1)
                if i >= 2:
                    act.wait_ge(s_sout, i - 1)
                act.activation(gsg[:, i % 2, :], bank[i % 4][:, :], ACT.Sigmoid).then_inc(s_gs, 1)
            act.wait_ge(s_vr, 1)
            act.activation(st[:, 0, 0, :], st[:, 0, 1, :], ACT.Sqrt).then_inc(s_sd, 1)
            for i in range(UT):
                act.wait_ge(s_yn, i + 1)
                act.activation(hT[:, 4 + i, :], cv[:, i, :], ACT.Silu, bias=dcol[:, 3, i:i + 1],
                               scale=dcol[:, 2, i:i + 1]).then_inc(s_lnout, 1)
            N2.act_all(act, s_xr, [2, 4, 6, 8])

        @block.vector
        def _(dve):
            ch = Chain(dve, s_chain)

            def V(i):
                return pv[:, i, :]

            def ts(o, a, s1, s2, op0, op1=ALU.bypass):
                ch.link(dve.tensor_scalar(o, a, s1, s2, op0, op1))

            def tt(o, a, b, op):
                ch.link(dve.tensor_tensor(o, a, b, op))

            def stt(o, a, s, b, op0, op1):
                ch.link(dve.scalar_tensor_tensor(o, a, s, b, op0, op1))

            MAGIC = 12582912.0

            def exp_small(o, a, n, r, t):
                ts(t, a, -87.0, 88.0, ALU.max, ALU.min)
                ts(n, t, 1.0 / math.log(2.0), MAGIC, ALU.mult, ALU.add)
                ts(n, n, MAGIC, None, ALU.subtract)
                stt(r, n, -0.693359375, t, ALU.mult, ALU.add)
                stt(r, n, 2.12194440e-4, r, ALU.mult, ALU.add)
                ts(t, r, 1.0 / math.factorial(8), None, ALU.mult)
                for q in range(7, 0, -1):
                    stt(t, t, 1.0 / math.factorial(q), r, ALU.add, ALU.mult)
                ts(t, t, 1.0, None, ALU.add)
                ts(n.bitcast(I32), n, 127.0, 8388608.0, ALU.add, ALU.mult)
                tt(o, t, n, ALU.mult)

            for b in range(NB):
                N.dve_scale(dve, b)

            dve.wait_ge(s_par, 80)
            lre, lim = sp[:, 0, :], sp[:, 1, :]
            exp_small(V(0), sp[:, 2, :], V(1), V(2), V(3))
            tt(V(4), lre, V(0), ALU.mult)
            exp_small(V(5), V(4), V(6), V(7), V(8))
            tt(V(9), lim, V(0), ALU.mult)
            ts(V(10), V(9), 1.0 / (2 * math.pi), MAGIC, ALU.mult, ALU.add)
            ts(V(11), V(10), MAGIC, None, ALU.subtract)
            c1 = 6.28125
            c2 = float(np.float32(2 * math.pi - c1))
            c3 = 2 * math.pi - c1 - c2
            stt(V(12), V(11), -c1, V(9), ALU.mult, ALU.add)
            stt(V(13), V(11), -c2, V(12), ALU.mult, ALU.add)
            stt(V(14), V(11), -c3, V(13), ALU.mult, ALU.add)
            dve.tensor_scalar(V(15), V(14), 3.1415925, -3.1415925, ALU.min, ALU.max).then_inc(s_sin_in, 1)

            dve.wait_ge(s_sin, 2)
            stt(V(22), V(21), -2.0, V(21), ALU.mult, ALU.mult)
            ts(pw[:, 0, 0, :], V(22), 1.0, None, ALU.add)
            ts(pw[:, 1, 0, :], V(20), 1.0, None, ALU.mult)
            for j in range(8):
                tt(V(23), pw[:, 0, j, :], pw[:, 0, j, :], ALU.mult)
                tt(V(24), pw[:, 1, j, :], pw[:, 1, j, :], ALU.mult)
                tt(pw[:, 0, j + 1, :], V(23), V(24), ALU.subtract)
                stt(pw[:, 1, j + 1, :], pw[:, 0, j, :], 2.0, pw[:, 1, j, :], ALU.mult, ALU.mult)
            dve.memset(ec[:, :, 0:1], 1.0).then_inc(s_first, 1)
            dve.memset(es[:, :, 0:1], 0.0).then_inc(s_first, 1)
            dve.sem_inc(s_pow, 1)
            dve.wait_ge(s_first, 2)
            for j in range(9):
                n = 1 << j
                for a, m in ([(0, n)] if n <= 128 else [(o, 128) for o in range(0, n, 128)]):
                    t = tmp_c[:, 0:NST * m].rearrange("p (k t) -> p k t", k=NST)
                    pc = bc(pw[:, 0, j, :].unsqueeze(2), [P, NST, m])
                    ps = bc(pw[:, 1, j, :].unsqueeze(2), [P, NST, m])
                    dve.wait_ge(s_es, j)
                    dve.tensor_tensor(ec[:, :, n + a:n + a + m], ec[:, :, a:a + m], pc, ALU.mult).then_inc(s_chain, 1)
                    dve.tensor_tensor(t, es[:, :, a:a + m], ps, ALU.mult).then_inc(s_chain, 1)
                    ch.n += 2
                    dve.wait_ge(s_chain, ch.n)
                    tt(ec[:, :, n + a:n + a + m], ec[:, :, n + a:n + a + m], t, ALU.subtract)
                dve.sem_inc(s_ec, 1)

            ts(V(25), V(5), -1.0, None, ALU.add)
            tt(V(26), V(5), V(22), ALU.mult)
            tt(V(27), V(25), V(26), ALU.add)
            tt(V(28), V(5), V(20), ALU.mult)
            tt(V(29), lre, lre, ALU.mult)
            tt(V(30), lim, lim, ALU.mult)
            tt(V(31), V(29), V(30), ALU.add)
            ch.link(dve.reciprocal(V(32), V(31)))
            tt(V(33), V(27), lre, ALU.mult)
            tt(V(34), V(28), lim, ALU.mult)
            tt(V(35), V(33), V(34), ALU.add)
            tt(V(36), V(35), V(32), ALU.mult)
            tt(V(33), V(28), lre, ALU.mult)
            tt(V(34), V(27), lim, ALU.mult)
            tt(V(35), V(33), V(34), ALU.subtract)
            tt(V(37), V(35), V(32), ALU.mult)
            kr = bc(V(36).unsqueeze(2), [P, NST, 32])
            ki = bc(V(37).unsqueeze(2), [P, NST, 32])
            tt(cc[:, 1, :, :], cT[:, 1, :, :], ki, ALU.mult)
            tt(cc[:, 2, :, :], cT[:, 0, :, :], kr, ALU.mult)
            tt(cc[:, 0, :, :], cc[:, 2, :, :], cc[:, 1, :, :], ALU.subtract)
            tt(cc[:, 1, :, :], cT[:, 0, :, :], ki, ALU.mult)
            tt(cc[:, 2, :, :], cT[:, 1, :, :], kr, ALU.mult)
            stt(cc[:, 2, :, :], cc[:, 2, :, :], -1.0, cc[:, 1, :, :], ALU.mult, ALU.subtract)
            dve.sem_inc(s_coef, 1)

            for i in range(UT):
                dve.wait_ge(s_zact, UT + i + 1)
                dve.wait_ge(s_z, 4 + 2 * i + 2)
                dve.tensor_tensor(cv[:, i, :], bank[(5 + 2 * i) % 4][:, :], gsg[:, i % 2, :], ALU.mult)\
                   .then_inc(s_zdve, 1)
                dve.wait_ge(s_zdve, i + 1)
                dve.tensor_copy(vpad[0][:, i, PAD:], cv[:, i, :]).then_inc(s_vlo, 1)
            dve.wait_ge(s_vlo, UT)
            for i in range(UT):
                dve.tensor_tensor(vpad[1][:, i, PAD:], cv[:, i, :], vpad[0][:, i, PAD:], ALU.subtract)\
                   .then_inc(s_vlo, 1)

            dve.wait_ge(s_es, 9)
            for k in range(NST):
                mag = bc(pv[:, 5, k:k + 1], [P, SEQ])
                vre, vim = bank[2 * (k % 2)], bank[2 * (k % 2) + 1]
                dve.wait_ge(s_v, k + 1)
                dve.tensor_tensor(rot[:, 0, :], vre[:, :], ec[:, k, :], ALU.mult).then_inc(s_chain, 1)
                dve.tensor_tensor(rot[:, 1, :], vim[:, :], es[:, k, :], ALU.mult).then_inc(s_chain, 1)
                dve.tensor_tensor(rot[:, 2, :], vim[:, :], ec[:, k, :], ALU.mult).then_inc(s_chain, 1)
                dve.tensor_tensor(rot[:, 3, :], vre[:, :], es[:, k, :], ALU.mult).then_inc(s_chain, 1)
                dve.wait_ge(s_chain, ch.n + 2)
                dve.tensor_tensor(rot[:, 0, :], rot[:, 0, :], rot[:, 1, :], ALU.add).then_inc(s_chain, 1)
                dve.wait_ge(s_chain, ch.n + 4)
                dve.tensor_tensor(rot[:, 2, :], rot[:, 2, :], rot[:, 3, :], ALU.subtract).then_inc(s_chain, 1)
                dve.sem_inc(s_vused, 1)
                dve.wait_ge(s_chain, ch.n + 5)
                if k >= 2:
                    dve.wait_ge(s_pp, 2 * (k - 1))
                dve.tensor_tensor_scan(st[:, k % 2, 0, :], mag, rot[:, 0, :], 0.0, ALU.mult, ALU.add)\
                   .then_inc(s_state, 1)
                dve.wait_ge(s_chain, ch.n + 6)
                dve.tensor_tensor_scan(st[:, k % 2, 1, :], mag, rot[:, 2, :], 0.0, ALU.mult, ALU.add)\
                   .then_inc(s_state, 1)
                ch.n += 6
                if k >= 2:
                    dve.wait_ge(s_cmm, k - 1)
                dve.wait_ge(s_state, 2 * k + 1)
                dve.tensor_tensor(pr[:, k % 2, 0, :], st[:, k % 2, 0, :], ec[:, k, :], ALU.mult).then_inc(s_pd, 1)
                dve.wait_ge(s_state, 2 * k + 2)
                dve.tensor_tensor(pr[:, k % 2, 2, :], st[:, k % 2, 1, :], ec[:, k, :], ALU.mult).then_inc(s_pd, 1)
                if k % 4 == 2 and k > 2:
                    skip(dve, k // 4 - 1)
            skip(dve, UT - 1)

            dve.wait_ge(s_mean, 1)
            for i in range(UT):
                dve.tensor_tensor(cv[:, i, :], cv[:, i, :], bank[6][:, :], ALU.subtract).then_inc(s_cen, 1)
            for i in range(UT):
                dve.wait_ge(s_gs, i + 1)
                dve.tensor_tensor(hT[:, i, :], yg[:, i, :], gsg[:, i % 2, :], ALU.mult).then_inc(s_sout, 1)
            dve.wait_ge(s_var, 1)
            dve.tensor_scalar(st[:, 0, 1, :], bank[7][:, :], EPS, None, ALU.add).then_inc(s_vr, 1)
            dve.wait_ge(s_sd, 1)
            dve.reciprocal(st[:, 1, 0, :], st[:, 0, 0, :]).then_inc(s_rs, 1)
            dve.wait_ge(s_rs, 1)
            for i in range(UT):
                dve.tensor_tensor(cv[:, i, :], cv[:, i, :], st[:, 1, 0, :], ALU.mult).then_inc(s_yn, 1)
            for n in range(2 * NB):
                dve.wait_ge(s_o, n + 1)
                b, half = n // 2, n % 2
                xs = x[:, b, half * 512:(half + 1) * 512]
                dve.tensor_tensor(xs, xs, bank[n][:, :], ALU.add).then_inc(s_xr, 1)
                if half == 1:
                    N2.dve_scale(dve, b)

        @block.tensor
        def _(pe):
            pe.wait_ge(loaded, 16)
            for b in range(NB):
                N.pe_turn(pe, b)
            pe.wait_ge(N.hT_ready, 2 * NB)
            for n in range(NZ):
                pe.wait_ge(s_win[n % 4], 16 * (n // 4 + 1))
                if n >= 4:
                    m = n - 4
                    if m < 4:
                        pe.wait_ge(s_zact, m + 1)
                    elif m % 2 == 0:
                        pe.wait_ge(s_zact, 4 + (m - 4) // 2 + 1)
                    else:
                        pe.wait_ge(s_zdve, (m - 5) // 2 + 1)
                w = wring[:, n % 4, :].rearrange("p (k c) -> p k c", k=KD)
                for k in range(KD):
                    mm = pe.matmul(bank[n % 4][:, :], w[:, k, :], hT[:, k, :], start=(k == 0), stop=(k == KD - 1))
                mm.then_inc(s_z, 1)
                pe.wait_ge(s_z, n + 1)
                pe.sem_inc(s_wuse, 1)

            def inputs(k):
                if k == 0:
                    pe.wait_ge(s_zact, 2 * UT)
                    pe.wait_ge(s_zdve, UT)
                if k >= 2:
                    pe.wait_ge(s_vused, k - 1)
                c, r = k // 4, 32 * (k % 4)
                for part in range(2):
                    mm = pe.matmul(bank[2 * (k % 2) + part][:, :], bT[r:r + 32, part, c, :], uT[r:r + 32, c, :],
                                   start=True, stop=True, tile_position=(r, 0))
                mm.then_inc(s_v, 1)

            def outputs(k):
                c, r = k // 4, 32 * (k % 4)
                if k == 0:
                    pe.wait_ge(s_coef, 1)
                if k % 4 == 0 and c >= 2:
                    pe.wait_ge(s_yd, c - 1)
                pe.wait_ge(s_h, 2 * (k + 1))
                for part in range(2):
                    mm = pe.matmul(bank[4 + c % 2][r:r + 32, :], cc[:, 2 * part, k, :], pr[:, k % 2, 2 * part, :],
                                   start=(part == 0), stop=(part == 1), tile_position=(0, r))
                mm.then_inc(s_cmm, 1)

            def conv_taps(taps, upto):
                while taps < min(upto, UT * CONV_K):
                    i, j = taps // CONV_K, taps % CONV_K
                    if j == 0 and i >= 2:
                        pe.wait_ge(s_cv, i - 1)
                    if j == 0:
                        pe.wait_ge(s_vlo, UT + i + 1)
                    pe.wait_ge(s_diag, 2 * (taps + 1))
                    for w, v in ((0, 0), (1, 0), (0, 1)):
                        mm = pe.matmul(bank[6 + i % 2][:, :], diag[w][:, taps % 8, :], vpad[v][:, i, j:j + SEQ],
                                       start=(j == 0 and (w, v) == (0, 0)), stop=(j == CONV_K - 1 and v == 1))
                    mm.then_inc(s_tap, 1)
                    taps += 1
                return taps

            pe.wait_ge(s_par, 80)
            pe.wait_ge(s_pad, 2)
            inputs(0)
            taps = 0
            for k in range(NST):
                if k + 1 < NST:
                    inputs(k + 1)
                taps = conv_taps(taps, 8 * (k + 1))
                if k:
                    outputs(k - 1)
            outputs(NST - 1)

            pe.wait_ge(s_ones, 1)
            pe.wait_ge(s_cv, UT)
            for i in range(UT):
                mm = pe.matmul(bank[6][:, :], ones[:, :], cv[:, i, :], start=(i == 0), stop=(i == UT - 1))
            mm.then_inc(s_mean, 1)
            pe.wait_ge(s_yg, UT)
            for q in range(2):
                pe.wait_ge(s_win[(NZ + q) % 4], 16 * ((NZ + q) // 4 + 1))
            for i in range(UT):
                for k in range(UT):
                    w = wring[:, (NZ + k // 2) % 4, :].rearrange("p (k c) -> p k c", k=2)[:, k % 2, i * P:(i + 1) * P]
                    mm = pe.matmul(bank[i][:, :], w, yg[:, k, :], start=(k == 0), stop=(k == UT - 1))
                mm.then_inc(s_glu, 1)
            for i in range(UT):
                pe.wait_ge(s_sq, i + 1)
                mm = pe.matmul(bank[7][:, :], ones[:, :], rot[:, i, :], start=(i == 0), stop=(i == UT - 1))
            mm.then_inc(s_var, 1)
            def project(o, ks):
                b, half = o // 2, o % 2
                for k in ks:
                    mm = pe.matmul(bank[o][:, :], hT[:, k, b * P:(b + 1) * P], w_out[:, k, half * 512:(half + 1) * 512],
                                   start=(k == 0), stop=(k == KD - 1))
                if k == KD - 1:
                    mm.then_inc(s_o, 1)

            pe.wait_ge(s_wout, 16)
            pe.wait_ge(s_sout, UT)
            for o in range(2 * NB):
                if o == 4:
                    pe.wait_ge(s_yd, UT)
                if o == 6:
                    pe.wait_ge(s_cen, UT)
                if o == 7:
                    pe.wait_ge(s_vr, 1)
                project(o, range(UT))
            pe.wait_ge(s_lnout, UT)
            for b in range(NB):
                project(2 * b, range(UT, KD))
                project(2 * b + 1, range(UT, KD))
                if b == 1:
                    pe.wait_ge(s_xr, 2)
                if b:
                    N2.pe_turn(pe, b - 1)
            N2.pe_turn(pe, NB - 1)



def peer(nc, D, layer, x, h, hT, wq_both, stat, ident, iota, g_next, out=None):
    tag = f"p{layer}_"
    R = 8
    with ExitStack() as ctx:
        def sb(name, shape, dt=F32):
            return ctx.enter_context(nc.sbuf_tensor(tag + name, shape, dt))

        def two(name, shape, dt=F32):
            return [sb(f"{name}{p}", shape, dt) for p in range(2)]

        sem = Sems(nc, ctx, tag)
        g = sb("g", [P, DM])
        wq = [wq_both[:, c, :].rearrange("p (k c) -> p k c", k=KD) for c in range(2)]
        keys = two("keys", [P, PK])
        qT = two("qT", [P, SEQ])
        S = sb("S", [P, NB, 2, PK])
        urow, vrow = sb("urow", [P, R, DM]), sb("vrow", [P, R, DM])
        diag = two("diag", [P, TOPK, P])
        sc2 = sb("sc2", [P, 2, PK])
        tops, topi = sb("tops", [P, 2, TOPK]), sb("topi", [P, 2, TOPK], U32)
        topf = sb("topf", [P, 2, TOPK])
        cand, cand2 = sb("cand", [P, TOPK, TOPK]), sb("cand2", [P, TOPK, TOPK])
        best, bestc = two("best", [P, TOPK]), sb("bestc", [P, TOPK], U32)
        ab, abf = sb("ab", [P, 2, TOPK], U32), sb("abf", [P, 2, TOPK])
        hit = sb("hit", [P, 2, TOPK, TOPK])
        sel, flat = sb("sel", [P, 2, TOPK]), sb("flat", [P, TOPK])
        idu, idv = two("idu", [P, TOPK], I32), two("idv", [P, TOPK], I32)
        negm, esum, e = two("negm", [P, 1]), two("esum", [P, 1]), two("e", [P, TOPK])
        a, ga, w, rs = two("a", [P, TOPK]), two("ga", [P, TOPK]), two("w", [P, TOPK]), two("rs", [P, 1])
        bankA = ctx.enter_context(nc.psum_tensor(tag + "psA", [P, SEQ], F32))
        bankB = ctx.enter_context(nc.psum_tensor(tag + "psB", [P, SEQ], F32))
        hp = ctx.enter_context(nc.psum_tensor(tag + "hp", [P, DM], F32))
        acc = [ctx.enter_context(nc.psum_tensor(f"{tag}acc{p}", [P, DM], F32)) for p in range(2)]
        tp = [bankA[:, :].rearrange("p (a b) -> p a b", a=4), bankB[:, :].rearrange("p (a b) -> p a b", a=4)]

        s_wqfree = sem("wq_buffers_used")
        s_wq = [sem(f"wq{c}_loaded") for c in range(2)]
        s_keys = [sem(f"keys{c}_loaded") for c in range(2)]
        s_q, s_qT = sem("query_tile_done"), sem("query_tile_taken")
        s_sd, s_S = sem("score_tile_done"), sem("score_tile_taken")
        s_ufree, s_vfree = sem("u_slots_free"), sem("v_slots_free")
        s_ug = [sem(f"u_rows{i}_landed") for i in range(R)]
        s_vg = [sem(f"v_rows{i}_landed") for i in range(R)]
        s_h = sem("h_staged")
        s_idu, s_idv = sem("u_indices_ready"), sem("v_indices_ready")
        s_best, s_exp = sem("best_scores_ready"), sem("exponents_ready")
        s_gelu, s_w = sem("gelu_ready"), sem("weights_ready")
        s_dgfree, s_dg = sem("diagonal_buffers_free"), sem("diagonals_ready")
        s_accfree, s_acc = sem("sum_buffers_free"), sem("sums_ready")
        s_chain = sem("dve_chain")
        s_tick = {n: sem(f"{n}_waits_passed") for n in ("pool", "dve", "act")}
        s_q0, s_qT0 = sem("first_query_piece_done"), sem("first_query_piece_taken")
        s_sd0, s_S0 = sem("first_score_piece_done"), sem("first_score_piece_taken")
        s_xb, s_out = sem("x_block_done"), sem("out_stored")
        N = Norm(sem, "n", x, h, hT, stat, g[:, :], tp, ident[:, :])
        PIECES = (slice(0, P), slice(P, SEQ))
        utab = D["peer_u"].rearrange("l e d -> (l e) d")
        vtab = D["peer_v"].rearrange("l e d -> (l e) d")
        wq_d = D["w_q"][layer].rearrange("n p c -> (n p) c")
        keys_d = D["keysT"][layer].rearrange("n p c -> (n p) c")

        def held(eng, name, s, value):
            eng.wait_ge(s, value)
            eng.sem_inc(s_tick[name], 1)

        block = sem.block()

        @block.sync
        def _(sp):
            for c in range(2):
                sp.dma_start(keys[c][:, :], keys_d[c * P:(c + 1) * P, :]).then_inc(s_keys[c], 16)
                sp.sem_inc(s_wq[c], 16)
            sp.dma_start(g[:, :], g_next.to_broadcast([P, DM])).then_inc(N.g_loaded, 16)
            with sp.Fori(0, PH - 1) as hd:
                for c in range(2):
                    sp.wait_ge(s_wqfree, 2 * hd + c + 1)
                    row = bass.ds((2 * hd + 2 + c) * P, P)
                    sp.dma_start(wq_both[:, c, :], wq_d[row, :]).then_inc(s_wq[c], 16)
                    sp.dma_start(keys[c][:, :], keys_d[row, :]).then_inc(s_keys[c], 16)
            if out is not None:
                for b in range(NB):
                    sp.wait_ge(N.h_ready, b + 1)
                    sp.dma_start(out[b * P:(b + 1) * P, :], h[:, b, :]).then_inc(s_out, 16)
                sp.wait_ge(s_out, 16 * NB)

        @block.gpsimd
        def _(pool):
            def rows(p, k, slots, free, landed, ids, table, value):
                held(pool, "pool", free, value)
                pool.indirect_dma_start(slots[:, k % R, :], None, table,
                                        bass.IndirectOffsetOnAxis(ap=ids[p][:, k:k + 1], axis=0))\
                    .then_inc(landed[k % R], 16)

            def step(v, b, more):
                p = b % 2
                if more:
                    held(pool, "pool", s_idu, v + 2)
                held(pool, "pool", s_idv, v + 1)
                for k in range(TOPK):
                    if more:
                        rows(1 - p, k, urow, s_ufree, s_ug, idu, utab, 16 * v + 16 + k + 1)
                    rows(p, k, vrow, s_vfree, s_vg, idv, vtab, 16 * v + k + 1)

            pool.wait_ge(s_idu, 1)
            for k in range(TOPK):
                rows(0, k, urow, s_ufree, s_ug, idu, utab, k + 1)
            with pool.Fori(0, PH - 1) as hd:
                for b in range(NB):
                    step(4 * hd + b, b, True)
            for b in range(NB):
                step(4 * (PH - 1) + b, b, b < NB - 1)

        @block.scalar
        def _(act):
            def stage_h(v, b):
                held(act, "act", s_ufree, 16 * v + R)
                act.copy(hp[:, :], h[:, b, :]).then_inc(s_h, 1)

            def exponents(v, p):
                held(act, "act", s_best, v + 1)
                act.activation(e[p][:, :], best[p][:, :], ACT.Exp, bias=negm[p][:, 0:1],
                               accum_out=esum[p][:, 0:1]).then_inc(s_exp, 1)

            def take_queries(t, c):
                held(act, "act", s_q, t + 1)
                act.copy(qT[c][:, :], bankA[:, :]).then_inc(s_qT, 1)

            def weights(v, p):
                held(act, "act", s_ufree, 16 * v + 16 + R)
                act.activation(ga[p][:, :], a[p][:, :], ACT.Gelu).then_inc(s_gelu, 1)
                held(act, "act", s_dgfree, v + 1)
                held(act, "act", s_w, v + 1)
                for k in range(TOPK):
                    act.activation(diag[p][:, k, :], ident[:, :], ACT.Copy, scale=w[p][:, k:k + 1]).then_inc(s_dg, 1)

            def step(hd, b, last):
                v, p = 4 * hd + b, b % 2
                if not (last and b == NB - 1):
                    stage_h(v + 1, (b + 1) % NB)
                if not (last and b >= NB - 2):
                    exponents(v + 2, p)
                if b < 2 and not last:
                    take_queries(2 * hd + 2 + b, b)
                if not (last and b == NB - 1):
                    weights(v + 1, 1 - p)

            for n, cols in enumerate(PIECES):
                for c in range(2):
                    act.wait_ge(s_q0, 2 * n + c + 1)
                    act.copy(qT[c][:, cols], acc[0][:, c * SEQ:(c + 1) * SEQ][:, cols]).then_inc(s_qT0, 1)
            stage_h(0, 0)
            exponents(0, 0)
            exponents(1, 1)
            weights(0, 0)
            with act.Fori(0, PH - 1) as hd:
                for b in range(NB):
                    step(hd, b, False)
            for b in range(NB):
                step(PH - 1, b, True)
                N.act_sums(act, b, s_xb, b + 1)
                if b and out is None:
                    N.act_take(act, b - 1)
            if out is None:
                N.act_take(act, NB - 1)

        @block.vector
        def _(dve):
            ch = Chain(dve, s_chain)

            def both(f):
                for c in range(2):
                    f(c).then_inc(s_chain, 1)
                ch.n += 2
                dve.wait_ge(s_chain, ch.n)

            def take_scores(head):
                held(dve, "dve", s_sd, 2 * head + 2)
                for c, bank in enumerate((bankB, bankA)):
                    dve.tensor_copy(S[:, :, c, :], bank[:, :].rearrange("p (b k) -> p b k", b=NB)).then_inc(s_S, 1)
                held(dve, "dve", s_S, 2 * head + 2)

            def route(p, b):
                s = S[:, b, :, :]
                both(lambda c: dve.max(tops[:, c, 0:8], s[:, c, :]))
                both(lambda c: dve.max_index(topi[:, c, 0:8], tops[:, c, 0:8], s[:, c, :]))
                both(lambda c: dve.match_replace(sc2[:, c, :], tops[:, c, 0:8], s[:, c, :], -3.0e38))
                both(lambda c: dve.max(tops[:, c, 8:16], sc2[:, c, :]))
                both(lambda c: dve.max_index(topi[:, c, 8:16], tops[:, c, 8:16], sc2[:, c, :]))
                dve.tensor_copy(topf[:, :, :], topi[:, :, :]).then_inc(s_chain, 1)
                ch.n += 1
                ch.link(dve.tensor_tensor(cand[:, :, :], bc(tops[:, 0, :].unsqueeze(2), [P, TOPK, TOPK]),
                                          bc(tops[:, 1, :].unsqueeze(1), [P, TOPK, TOPK]), ALU.add))
                c1 = cand[:, :, :].rearrange("p a b -> p (a b)")
                c2 = cand2[:, :, :].rearrange("p a b -> p (a b)")
                ch.link(dve.max(best[p][:, 0:8], c1))
                ch.link(dve.max_index(bestc[:, 0:8], best[p][:, 0:8], c1))
                ch.link(dve.match_replace(c2, best[p][:, 0:8], c1, -3.0e38))
                ch.link(dve.max(best[p][:, 8:16], c2))
                ch.link(dve.max_index(bestc[:, 8:16], best[p][:, 8:16], c2))
                ch.link(dve.tensor_scalar(negm[p][:, :], best[p][:, 0:1], -1.0, None, ALU.mult))
                dve.sem_inc(s_best, 1)
                ch.link(dve.tensor_scalar(ab[:, 0, :], bestc[:, :], 4, None, ALU.logical_shift_right))
                ch.link(dve.tensor_scalar(ab[:, 1, :], bestc[:, :], 15, None, ALU.bitwise_and))
                ch.link(dve.tensor_copy(abf[:, :, :], ab[:, :, :]))
                ch.link(dve.tensor_tensor(hit[:, :, :, :], bc(abf[:, :, :].unsqueeze(3), [P, 2, TOPK, TOPK]),
                                          bc(iota[:, :].unsqueeze(1).unsqueeze(1), [P, 2, TOPK, TOPK]), ALU.is_equal))
                ch.link(dve.tensor_tensor(hit[:, :, :, :], hit[:, :, :, :],
                                          bc(topf[:, :, :].unsqueeze(2), [P, 2, TOPK, TOPK]), ALU.mult))
                ch.link(dve.tensor_reduce(sel[:, :, :], hit[:, :, :, :], AX_X, ALU.add))
                ch.link(dve.scalar_tensor_tensor(flat[:, :], sel[:, 0, :], float(PK), sel[:, 1, :], ALU.mult, ALU.add))
                ch.link(dve.tensor_scalar(idu[p][:, :], flat[:, :], float(layer * NEXP), None, ALU.add))
                dve.sem_inc(s_idu, 1)

            def v_indices(p):
                ch.link(dve.tensor_copy(idv[p][:, :], idu[p][:, :]))
                dve.sem_inc(s_idv, 1)

            def dots(v, p):
                held(dve, "dve", s_h, v + 1)
                for k in range(TOPK):
                    dve.wait_ge(s_ug[k % R], 32 * v + 16 * (k // R + 1))
                    dve.tensor_tensor_reduce(urow[:, k % R, :], urow[:, k % R, :], hp[:, :], 1.0, 0.0,
                                             ALU.mult, ALU.add, a[p][:, k:k + 1]).then_inc(s_ufree, 1)
                held(dve, "dve", s_exp, v + 1)
                ch.link(dve.reciprocal(rs[p][:, :], esum[p][:, :]))
                held(dve, "dve", s_gelu, v + 1)
                ch.link(dve.scalar_tensor_tensor(w[p][:, :], ga[p][:, :], rs[p][:, 0:1], e[p][:, :],
                                                 ALU.mult, ALU.mult))
                dve.sem_inc(s_w, 1)

            def step(hd, b, last):
                v, p = 4 * hd + b, b % 2
                dve.sem_clear(s_chain)
                ch.n = 0
                if not (last and b == NB - 1):
                    v_indices(1 - p)
                if b == 2 and not last:
                    take_scores(hd + 1)
                if not (last and b >= NB - 2):
                    route(p, (b + 2) % NB)
                if not (last and b == NB - 1):
                    dots(v + 1, 1 - p)
                held(dve, "dve", s_acc, v + 1)
                ch.link(dve.tensor_tensor(x[:, b, :], x[:, b, :], acc[p][:, :], ALU.add))
                dve.sem_inc(s_accfree, 1)
                if last:
                    dve.sem_inc(s_xb, 1)
                    N.dve_scale(dve, b)

            dve.sem_inc(s_ufree, R)
            dve.sem_inc(s_accfree, 2)
            def take_first(n, blocks):
                for c, bank in enumerate((bankB, bankA)):
                    dve.wait_ge(s_sd0, 2 * n + c + 1)
                    dve.tensor_copy(S[:, blocks, c, :],
                                    bank[:, :].rearrange("p (b k) -> p b k", b=NB)[:, blocks, :]).then_inc(s_S0, 1)
                dve.wait_ge(s_S0, 2 * n + 2)

            take_first(0, slice(0, 1))
            route(0, 0)
            take_first(1, slice(1, NB))
            dve.sem_inc(s_S, 2)
            route(1, 1)
            v_indices(0)
            dots(0, 0)
            with dve.Fori(0, PH - 1) as hd:
                for b in range(NB):
                    step(hd, b, False)
            for b in range(NB):
                step(PH - 1, b, True)

        @block.tensor
        def _(pe):
            def queries(head, c):
                pe.wait_ge(s_wq[c], 16 * (head + 1))
                if c == 1:
                    pe.wait_ge(s_qT, 2 * head + 1)
                else:
                    pe.wait_ge(s_S, 2 * head)
                for k in range(KD):
                    mm = pe.matmul(bankA[:, :], wq[c][:, k, :], hT[:, k, :], start=(k == 0), stop=(k == KD - 1))
                mm.then_inc(s_q, 1)

            def scores(head, c):
                pe.wait_ge(s_keys[c], 16 * (head + 1))
                pe.wait_ge(s_qT, 2 * head + c + 1)
                for b in range(NB):
                    mm = pe.matmul((bankB, bankA)[c][:, b * PK:(b + 1) * PK], qT[c][:, b * P:(b + 1) * P],
                                   keys[c][:, :], start=True, stop=True, skip_group_check=True)
                mm.then_inc(s_sd, 1)

            def release(head, c):
                pe.wait_ge(s_sd, 2 * head + c + 1)
                pe.sem_inc(s_wqfree, 1)

            def step(hd, b, last):
                v, p = 4 * hd + b, b % 2
                if b == 0 and not last:
                    queries(hd + 1, 0)
                if b == 1 and not last:
                    scores(hd + 1, 0)
                    queries(hd + 1, 1)
                pe.wait_ge(s_accfree, v + 1)
                for k in range(TOPK):
                    if k == TOPK // 2 and b == 1 and not last:
                        scores(hd + 1, 1)
                    if k == TOPK // 2 and last and b and out is None:
                        N.pe_turn(pe, b - 1)
                    pe.wait_ge(s_dg, 16 * v + k + 1)
                    pe.wait_ge(s_vg[k % R], 32 * v + 16 * (k // R + 1))
                    for half in range(2):
                        mm = pe.matmul(acc[p][:, half * 512:(half + 1) * 512], diag[p][:, k, :],
                                       vrow[:, k % R, half * 512:(half + 1) * 512],
                                       start=(k == 0), stop=(k == TOPK - 1))
                    mm.then_inc(s_vfree, 1)
                pe.wait_ge(s_vfree, 16 * v + 16 + R)
                pe.sem_inc(s_acc, 1)
                pe.sem_inc(s_dgfree, 1)
                if b == 1 and not last:
                    for c in range(2):
                        release(hd + 1, c)

            for n, cols in enumerate(PIECES):
                for c in range(2):
                    pe.wait_ge(s_wq[c], 16)
                    for k in range(KD):
                        mm = pe.matmul(acc[0][:, c * SEQ:(c + 1) * SEQ][:, cols], wq[c][:, k, :], hT[:, k, cols],
                                       start=(k == 0), stop=(k == KD - 1), skip_group_check=True)
                    mm.then_inc(s_q0, 1)
                for c in range(2):
                    pe.wait_ge(s_keys[c], 16)
                    pe.wait_ge(s_qT0, 2 * n + c + 1)
                    if n:
                        pe.wait_ge(s_S0, 2)
                    for b in (range(1), range(1, NB))[n]:
                        mm = pe.matmul((bankB, bankA)[c][:, b * PK:(b + 1) * PK], qT[c][:, b * P:(b + 1) * P],
                                       keys[c][:, :], start=True, stop=True, skip_group_check=True)
                    mm.then_inc(s_sd0, 1)
            pe.wait_ge(s_sd0, 4)
            pe.sem_inc(s_q, 2)
            pe.sem_inc(s_qT, 2)
            pe.sem_inc(s_sd, 2)
            pe.sem_inc(s_wqfree, 2)
            pe.sem_inc(s_vfree, R)
            pe.sem_inc(s_dgfree, 2)
            with pe.Fori(0, PH - 1) as hd:
                for b in range(NB):
                    step(hd, b, False)
            for b in range(NB):
                step(PH - 1, b, True)
            if out is None:
                N.pe_turn(pe, NB - 1)



def attention_mixer(nc, D, x, h, hT, wq, stat, ident):
    QUADS = NB * NH // 4
    SLOT = (0, 2, 1, 3)
    with ExitStack() as ctx:
        def sb(name, shape, dt=F32):
            return ctx.enter_context(nc.sbuf_tensor("at_" + name, shape, dt))

        sem = Sems(nc, ctx, "at_")

        g = sb("g", [P, DM])
        wqkv = sb("wqkv", [P, KD, QKV])
        wo = sb("wo", [P, KD, DM])
        bias = sb("bias", [P, QKV])
        cs = sb("cos_sin", [P, 2, NB, ROT])
        sinks = sb("sinks", [P, NH])
        mask = sb("mask", [P, 2, 2 * P])
        qk = sb("qk", [P, NB, NH + NKV, HD])
        kd = sb("kd", [P, NB, NKV, 2, HD])
        v = sb("v", [P, NB + 1, NKV * HD])
        rt = sb("rope_tmp", [P, 4, NH + NKV, ROT])
        qT = sb("qT", [P, NB, KD, P])
        kT = sb("kT", [P, NKV, P + SEQ])
        sc = sb("scores", [P, 2, 4, 2 * P])
        pe_ = wq[:, :, :].rearrange("p n (j k) -> p n j k", j=4)
        pT = sb("probsT", [P, 2, 8, P])
        sm = sb("softmax_cols", [P, 2, 8, 4])
        bank = [ctx.enter_context(nc.psum_tensor(f"at_ps{i}", [P, 2, 512], F32)) for i in range(4)]

        def B(i):
            return bank[i // 2][:, i % 2, :]

        tp = [B(0).rearrange("p (a b) -> p a b", a=4), B(1).rearrange("p (a b) -> p a b", a=4)]
        s_w = [sem(f"wqkv_part{i}_loaded") for i in range(6)]
        s_wq = sem("first_query_weights_loaded")
        s_wo, s_c = sem("wo_loaded"), sem("constants_loaded")
        s_pad = sem("padding_zeroed")
        s_p, s_pt = sem("qkv_piece_done"), sem("qkv_piece_taken")
        s_chain = sem("dve_chain")
        s_rope = sem("block_rotated")
        s_tq, s_tqt = sem("qk_turned"), sem("qk_turned_taken")
        s_s, s_sm, s_nm = sem("scores_done"), sem("scores_masked"), sem("maximum_ready")
        s_e, s_pn = sem("exponents_ready"), sem("probs_ready")
        s_tpd, s_tpt = sem("probs_turned"), sem("probs_turned_taken")
        s_pv, s_pvt = sem("pv_done"), sem("pv_taken")
        s_o, s_xr = sem("out_block_done"), sem("residual_added")
        N = Norm(sem, "n", x, h, hT, stat, g[:, :], tp, ident[:, :])
        PIECES = [(0, 512), (512, 512), (1024, 256)]
        BESIDE = {0: ("qkv", 6), 1: ("qkv", 7), 2: ("qkv", 8), 4: ("qkv", 9), 5: ("qkv", 10), 6: ("qkv", 11),
                  7: ("out", 0), 8: ("out", 1), 9: ("out", 2), 10: ("out", 3), 13: ("out", 4), 14: ("out", 5)}
        AHEAD = 2 * len(PIECES)

        def piece_bank(m):
            return B(m % 4 if m < AHEAD else 7)

        def out_bank(o):
            return B(6 if o == 2 * NB - 1 else 7)

        block = sem.block()

        @block.sync
        def _(sp):
            w_d = D["w_qkv"].rearrange("(k p) c -> p k c", p=P)
            for q, (c0, cn) in enumerate(PIECES):
                for k in (0, KD // 2):
                    sp.dma_start(wqkv[:, k:k + KD // 2, c0:c0 + cn], w_d[:, k:k + KD // 2, c0:c0 + cn])\
                      .then_inc(s_w[2 * q + 2 * k // KD], 16)
            sp.dma_start(bias[:, :], D["b_qkv"].to_broadcast([P, QKV])).then_inc(s_c, 16)
            sp.dma_start(cs[:, :, :, :], D["rope"]).then_inc(s_c, 16)
            sp.dma_start(sinks[:, :], D["sinks"].to_broadcast([P, NH])).then_inc(s_c, 16)
            sp.dma_start(mask[:, :, :], D["masks"]).then_inc(s_c, 16)
            sp.dma_start(wo[:, :, :], D["w_o"].rearrange("(k p) c -> p k c", p=P)).then_inc(s_wo, 16)
            sp.dma_start(g[:, :], D["g_ffn"][1:2, :].to_broadcast([P, DM])).then_inc(N.g_loaded, 16)
            first_queries(sp, D, 1, wq, s_tpd, QUADS, s_wq)
            sp.wait_ge(s_wq, 16)

        @block.gpsimd
        def _(pool):
            pool.memset(kT[:, :, 0:P], 0.0).then_inc(s_pad, 1)
            pool.memset(v[:, 0, :], 0.0).then_inc(s_pad, 1)

        @block.scalar
        def _(act):
            def take_qk(b):
                for q in range(2):
                    act.wait_ge(s_tq, 3 * b + q + 1)
                    act.copy(qT[:, b, 4 * q:4 * q + 4, :].rearrange("p a t -> p (a t)"), B(4 + q)).then_inc(s_tqt, 1)
                act.wait_ge(s_tq, 3 * b + 3)
                act.copy(kT[:, :, P + b * P:P + (b + 1) * P],
                         B(7)[:, 0:2 * P].rearrange("p (g t) -> p g t", g=2)).then_inc(s_tqt, 1)

            def exps(n):
                act.wait_ge(s_nm, n + 1)
                if n >= 2:
                    act.wait_ge(s_tpd, n - 1)
                for j in range(4):
                    act.activation(pe_[:, n % 2, j, :], sc[:, n % 2, j, :], ACT.Exp, bias=sm[:, n % 2, 2, j:j + 1],
                                   accum_out=sm[:, n % 2, 5, j:j + 1]).then_inc(s_e, 1)
                act.activation(sm[:, n % 2, 4, :], sm[:, n % 2, 3, :], ACT.Exp).then_inc(s_e, 1)

            def take_turned(n):
                act.wait_ge(s_tpd, n + 1)
                if n >= 2:
                    act.wait_ge(s_pv, n - 1)
                act.copy(pT[:, n % 2, :, :].rearrange("p (a c) t -> p a (c t)", a=2), bank[2][:, :, :]).then_inc(s_tpt, 1)

            def take_outputs(n):
                act.wait_ge(s_pv, n + 1)
                b, quad = n // 4, n % 4
                act.copy(hT[:, 2 * quad:2 * quad + 2, b * P:(b + 1) * P],
                         B(6)[:, 0:2 * P].rearrange("p (m t) -> p m t", m=2)).then_inc(s_pvt, 1)

            take_qk(0)
            exps(0)
            for n in range(QUADS):
                if n + 1 < QUADS:
                    exps(n + 1)
                take_turned(n)
                if n:
                    take_outputs(n - 1)
                if n % 4 == 1 and n // 4 + 1 < NB:
                    take_qk(n // 4 + 1)
            take_outputs(QUADS - 1)
            for b in range(NB - 1):
                N.act_sums(act, b, s_xr, 2 * b + 2)
            for b in range(NB - 1):
                N.act_take(act, b)
            N.act_sums(act, NB - 1, s_xr, 2 * NB)
            N.act_take(act, NB - 1)

        @block.vector
        def _(dve):
            ch = Chain(dve, s_chain)
            dve.wait_ge(s_c, 64)
            def take_piece(m):
                b, q = m // len(PIECES), m % len(PIECES)
                c0, cn = PIECES[q]
                dve.wait_ge(s_p, m + 1)
                ps = piece_bank(m)
                if q < 2:
                    dve.tensor_tensor(qk[:, b, 8 * q:8 * q + 8, :].rearrange("p n d -> p (n d)"), ps,
                                      bias[:, c0:c0 + cn], ALU.add).then_inc(s_pt, 1)
                else:
                    dve.tensor_tensor(qk[:, b, NH:, :].rearrange("p n d -> p (n d)"), ps[:, 0:P],
                                      bias[:, c0:c0 + P], ALU.add).then_inc(s_chain, 1)
                    ch.n += 1
                    dve.tensor_tensor(v[:, b + 1, :], ps[:, P:2 * P], bias[:, c0 + P:c0 + 2 * P],
                                      ALU.add).then_inc(s_pt, 1)
                    rotate(b)

            def rotate(b):
                dve.wait_ge(s_pt, 3 * b + 3)
                dve.wait_ge(s_chain, ch.n)
                x1, x2 = qk[:, b, :, 0:ROT], qk[:, b, :, ROT:2 * ROT]
                co = bc(cs[:, 0, b, :].unsqueeze(1), [P, NH + NKV, ROT])
                si = bc(cs[:, 1, b, :].unsqueeze(1), [P, NH + NKV, ROT])
                for t, (u, w) in enumerate(((x1, co), (x2, si), (x2, co), (x1, si))):
                    dve.tensor_tensor(rt[:, t, :, :], u, w, ALU.mult).then_inc(s_chain, 1)
                ch.n += 4
                dve.wait_ge(s_chain, ch.n)
                dve.tensor_tensor(x1, rt[:, 0, :, :], rt[:, 1, :, :], ALU.subtract).then_inc(s_chain, 1)
                dve.tensor_tensor(x2, rt[:, 2, :, :], rt[:, 3, :, :], ALU.add).then_inc(s_chain, 1)
                ch.n += 2
                dve.wait_ge(s_chain, ch.n)
                dve.tensor_copy(kd[:, b, :, :, :], bc(qk[:, b, NH:, :].unsqueeze(2), [P, NKV, 2, HD])).then_inc(s_rope, 1)

            def add_out(o):
                dve.wait_ge(s_o, o + 1)
                b, half = o // 2, o % 2
                xs = x[:, b, half * 512:(half + 1) * 512]
                dve.tensor_tensor(xs, xs, out_bank(o), ALU.add).then_inc(s_xr, 1)

            def front(n):
                b, quad = n // 4, n % 4
                dve.wait_ge(s_s, n + 1)
                if n >= 2:
                    dve.wait_ge(s_e, 5 * (n - 1))
                dve.scalar_tensor_tensor(sc[:, n % 2, :, :], bank[n % 2][:, :, :].rearrange("p a (c k) -> p (a c) k", c=2),
                                         HD ** -0.5, bc(mask[:, min(b, 1), :].unsqueeze(1), [P, 4, 2 * P]),
                                         ALU.mult, ALU.add).then_inc(s_sm, 1)
                dve.wait_ge(s_sm, n + 1)
                c = sm[:, n % 2, :, :]
                sk = sinks[:, 4 * quad:4 * quad + 4]
                ch.link(dve.tensor_reduce(c[:, 0, :], sc[:, n % 2, :, :], AX_X, ALU.max))
                ch.link(dve.tensor_tensor(c[:, 1, :], c[:, 0, :], sk, ALU.max))
                ch.link(dve.tensor_tensor(c[:, 3, :], sk, c[:, 1, :], ALU.subtract))
                dve.tensor_scalar(c[:, 2, :], c[:, 1, :], -1.0, None, ALU.mult).then_inc(s_nm, 1)

            def back(n):
                dve.wait_ge(s_e, 5 * (n + 1))
                c = sm[:, n % 2, :, :]
                ch.link(dve.tensor_tensor(c[:, 6, :], c[:, 5, :], c[:, 4, :], ALU.add))
                ch.link(dve.reciprocal(c[:, 7, :], c[:, 6, :]))
                dve.tensor_tensor(pe_[:, n % 2, :, :], pe_[:, n % 2, :, :],
                                  bc(c[:, 7, :].unsqueeze(2), [P, 4, 2 * P]), ALU.mult).then_inc(s_pn, 1)

            for m in range(AHEAD):
                take_piece(m)
            front(0)
            for n in range(QUADS):
                if n + 1 < QUADS:
                    front(n + 1)
                back(n)
                kind, i = BESIDE.get(n - 1, ("", 0))
                if kind == "qkv":
                    take_piece(i)
                elif kind == "out":
                    add_out(i)
            for b in range(NB - 1):
                N.dve_scale(dve, b)
            for o in (2 * NB - 2, 2 * NB - 1):
                add_out(o)
            N.dve_scale(dve, NB - 1)

        @block.tensor
        def _(pe):
            def project(m):
                b, q = m // len(PIECES), m % len(PIECES)
                c0, cn = PIECES[q]
                if 4 <= m < AHEAD:
                    pe.wait_ge(s_pt, m - 3)
                for k in range(KD):
                    if b == 0 and k % (KD // 2) == 0:
                        pe.wait_ge(s_w[2 * q + 2 * k // KD], 16)
                    mm = pe.matmul(piece_bank(m)[:, 0:cn], hT[:, k, b * P:(b + 1) * P], wqkv[:, k, c0:c0 + cn],
                                   start=(k == 0), stop=(k == KD - 1))
                mm.then_inc(s_p, 1)

            def project_out(o):
                b, half = o // 2, o % 2
                pe.wait_ge(s_pvt, 4 * (b + 1))
                pe.wait_ge(s_wo, 16)
                for k in range(KD):
                    mm = pe.matmul(out_bank(o), hT[:, k, b * P:(b + 1) * P], wo[:, k, half * 512:(half + 1) * 512],
                                   start=(k == 0), stop=(k == KD - 1))
                mm.then_inc(s_o, 1)

            def bank7_free(n):
                past = [BESIDE[i] for i in BESIDE if i < n]
                if past:
                    kind, i = past[-1]
                    pe.wait_ge(s_pt if kind == "qkv" else s_xr, i + 1)

            def turn(b, n):
                pe.wait_ge(s_rope, b + 1)
                if b:
                    pe.wait_ge(s_tpt, n + 1)
                bank7_free(n)
                for q in range(2):
                    for t in range(4):
                        m = 4 * q + t
                        mm = pe.transpose(B(4 + q)[:, t * P:(t + 1) * P],
                                          qk[:, b, 2 * m:2 * m + 2, :].rearrange("p n d -> p (n d)"), ident[:, :])
                    mm.then_inc(s_tq, 1)
                for t in range(NKV):
                    mm = pe.transpose(B(7)[:, t * P:(t + 1) * P], kd[:, b, t, :, :].rearrange("p n d -> p (n d)"),
                                      ident[:, :])
                mm.then_inc(s_tq, 1)

            def scores(n):
                b, quad = n // 4, n % 4
                if n == 0:
                    pe.wait_ge(s_pt, AHEAD)
                if n % 4 == 0:
                    pe.wait_ge(s_tqt, 3 * (b + 1))
                if n >= 2:
                    pe.wait_ge(s_sm, n - 1)
                for j in range(4):
                    hq = 4 * quad + j
                    r, grp = 64 * (hq % 2), hq // (NH // NKV)
                    mm = pe.matmul(bank[n % 2][:, j % 2, (j // 2) * 2 * P:(j // 2 + 1) * 2 * P],
                                   qT[r:r + 64, b, hq // 2, :], kT[r:r + 64, grp, b * P:(b + 2) * P],
                                   start=True, stop=True, skip_group_check=True, tile_position=(r, 0))
                mm.then_inc(s_s, 1)

            def turn_probs(n):
                pe.wait_ge(s_pn, n + 1)
                if n:
                    pe.wait_ge(s_tpt, n)
                if n % 4 == 2 and n // 4 + 1 < NB:
                    pe.wait_ge(s_tqt, 3 * (n // 4 + 2))
                for t in range(8):
                    mm = pe.transpose(bank[2][:, t // 4, (t % 4) * P:(t % 4 + 1) * P],
                                      pe_[:, n % 2, t // 2, (t % 2) * P:(t % 2 + 1) * P], ident[:, :])
                mm.then_inc(s_tpd, 1)

            def outputs(n):
                b, quad = n // 4, n % 4
                pe.wait_ge(s_tpt, n + 1)
                if n:
                    pe.wait_ge(s_pvt, n)
                for j in range(4):
                    hq = 4 * quad + j
                    r, grp = 64 * (hq % 2), hq // (NH // NKV)
                    for side in range(2):
                        mm = pe.matmul(B(6)[r:r + 64, (j // 2) * P:(j // 2 + 1) * P],
                                       v[:, b + side, grp * HD:(grp + 1) * HD], pT[:, n % 2, 2 * SLOT[j] + side, :],
                                       start=(side == 0), stop=(side == 1), tile_position=(0, r))
                mm.then_inc(s_pv, 1)

            pe.wait_ge(s_pad, 2)
            for m in range(AHEAD):
                project(m)
                if m == 3:
                    turn(0, 0)
            scores(0)
            scores(1)
            for n in range(QUADS):
                turn_probs(n)
                if n + 2 < QUADS:
                    scores(n + 2)
                if n:
                    outputs(n - 1)
                if n % 4 == 1 and n // 4 + 1 < NB:
                    turn(n // 4 + 1, n)
                kind, i = BESIDE.get(n, ("", 0))
                if kind:
                    bank7_free(n)
                    turned = min((n + 3) // 4 + 1, NB)
                    pe.wait_ge(s_tqt, 3 * turned)
                if kind == "qkv":
                    project(i)
                elif kind == "out":
                    project_out(i)
            outputs(QUADS - 1)
            bank7_free(QUADS)
            project_out(2 * NB - 2)
            pe.wait_ge(s_sm, QUADS)
            for b in range(NB - 1):
                N.pe_turn(pe, b)
            project_out(2 * NB - 1)
            N.pe_turn(pe, NB - 1)


def build(nc, D, out):
    with ExitStack() as ctx:
        x = ctx.enter_context(nc.sbuf_tensor("x_res", [P, NB, DM], F32))
        ident = ctx.enter_context(nc.sbuf_tensor("ident", [P, P], F32))
        loaded = ctx.enter_context(nc.semaphore("ident_loaded"))
        iota = ctx.enter_context(nc.sbuf_tensor("iota16", [P, TOPK], F32))
        stat = ctx.enter_context(nc.sbuf_tensor("norm_stat", [P, 4, NB], F32))
        h = ctx.enter_context(nc.sbuf_tensor("h", [P, NB, DM], F32))
        with nc.sbuf_tensor("m0_vpad_lo", [P, UT, CONV_K - 1 + SEQ], F32R) as vpad_lo, \
                nc.sbuf_tensor("m0_diag_lo", [P, 8, P], F32R) as diag_lo:
            low = (vpad_lo, diag_lo)
        hT = ctx.enter_context(nc.sbuf_tensor("hT", [P, KD, SEQ], F32))
        wq = ctx.enter_context(nc.sbuf_tensor("wq", [P, 2, KD * P], F32))
        hybrid_mixer(nc, D, x, h, hT, wq, low, stat, ident, loaded, iota)
        peer(nc, D, 0, x, h, hT, wq, stat, ident, iota, D["g_mix"][1:2, :])
        attention_mixer(nc, D, x, h, hT, wq, stat, ident)
        peer(nc, D, 1, x, h, hT, wq, stat, ident, iota, D["g_fin"], out)


def kernel(**inputs):
    import concourse.bacc as _bacc
    from concourse.bass_utils import run_bass_kernel_spmd as _run
    a = {k: np.asarray(v) for k, v in inputs.items()}
    f = np.float32

    def tiles(v, n):
        return v.reshape(n, P).T

    G2 = (S5_G // 2, 2)
    re, im = a["s5_lambda_re"][0], a["s5_lambda_im"][0]
    step = np.broadcast_to(a["s5_log_step"][0][:, None], (S5_G, S5_P))
    scal = np.stack([tiles(re, NST), tiles(im, NST), tiles(step, NST)], 1)
    bT = np.zeros((2, UT, 4, 2, S5_H, 2, S5_P), f)
    cT = np.zeros((2, NST, 2, S5_P, 2, S5_H), f)
    for part, (bn, cn) in enumerate((("s5_b_re", "s5_c_re"), ("s5_b_im", "s5_c_im"))):
        b = a[bn][0].reshape(UT, 4, 2, S5_P, S5_H)
        c = a[cn][0].reshape(NST, 2, S5_H, S5_P)
        for q in range(2):
            bT[part, :, :, q, :, q, :] = b[:, :, q].transpose(0, 1, 3, 2)
            cT[part, :, q, :, q, :] = c[:, q].transpose(0, 2, 1)
    bT = bT.reshape(2, UT, P, P).transpose(2, 0, 1, 3)
    cT = cT.reshape(2, NST, P, 32).transpose(2, 0, 1, 3)
    cols = np.stack([tiles(a[n][0].reshape(-1), UT) for n in ("s5_d", "conv_dw_b", "conv_ln_g", "conv_ln_b")], 1)
    conv_w = a["conv_dw_w"][0].T.reshape(UT, P, CONV_K).transpose(1, 0, 2)

    keysT = a["peer_sub_keys"].reshape(2, NQT, PK, P).transpose(0, 1, 3, 2)
    w_q = a["peer_w_q"].reshape(2, KD, P, NQT, P).transpose(0, 3, 2, 1, 4).reshape(2, NQT, P, DM)
    inv = np.power(f(500000.0), -np.arange(0, 2 * ROT, 2, dtype=f) / f(2 * ROT)).astype(f)
    ang = np.arange(SEQ, dtype=f)[:, None] * inv[None, :]
    rope = np.stack([np.cos(ang), np.sin(ang)]).astype(f).reshape(2, NB, P, ROT).transpose(2, 0, 1, 3)
    diff = P + np.arange(P)[:, None] - np.arange(2 * P)[None, :]
    band = (diff >= 0) & (diff < P)
    masks = np.stack([np.where(band & (np.arange(2 * P) >= P), 0.0, NEG), np.where(band, 0.0, NEG)], 1).astype(f)
    sinks = a["attn_sinks"].reshape(NH // 4, 2, 2).transpose(0, 2, 1).reshape(1, NH)
    D = {"w_qkv": a["attn_w_qkv"][0], "b_qkv": a["attn_b_qkv"], "sinks": sinks, "w_o": a["attn_w_o"][0],
         "rope": rope, "masks": masks, "g_fin": a["norm_final"][None],
         "keysT": keysT, "w_q": w_q, "g_ffn": a["norm_ffn"], "peer_u": a["peer_u"], "peer_v": a["peer_v"],
         "x": a["x"][0], "ident": np.eye(P, dtype=f), "g_mix": a["norm_mix"],
         "s5_scal": scal, "s5_bT": bT, "s5_cT": cT, "chan_cols": cols, "conv_w": conv_w,
         "w_in": a["mix_w_in"][0], "w_glu": a["s5_w_glu"][0], "w_out": a["mix_w_out"][0]}

    nc = _bacc.Bacc("TRN2", target_bir_lowering=False, num_devices=1)
    arrays, aps = {}, {}
    for name, v in D.items():
        v = np.ascontiguousarray(v)
        arrays[f"in_{name}"] = v
        aps[name] = nc.dram_tensor(f"in_{name}", v.shape, mybir.dt.from_np(v.dtype), kind="ExternalInput").ap()
    out = nc.dram_tensor("out", (SEQ, DM), F32, kind="ExternalOutput").ap()
    build(nc, aps, out)
    r = _run(nc, [arrays], core_ids=[0])
    return r.results[0]["out"].reshape(1, SEQ, DM)
```
